# Optimizing a Trainium2 kernel written in Bass

```python
import math
import jax
import jax.numpy as jnp
from jax import lax
import numpy as np

D_MODEL = 1024
BATCH = 1
SEQ = 1024
DEPTH = 1

GRID_W = 64
CTX_LEN = 256
EPS = 1e-6

CONV_CH = 256
CONV_WIDTH = 31
GDN_HEADS = 4
GDN_DK = 64
GDN_DV = 64
GDN_WIDTH = GDN_HEADS * GDN_DV
GDN_QKV = 2 * GDN_HEADS * GDN_DK + GDN_WIDTH
SHORT_CONV = 5
GDN_CHUNK = 64
HEAD_DIM = 64
ATTN_Q_HEADS = 8
ATTN_KV_HEADS = 2
ATTN_GROUP = ATTN_Q_HEADS // ATTN_KV_HEADS
ATTN_WIDTH = ATTN_Q_HEADS * HEAD_DIM
Q_BLOCK = 128
ROPE_THETA = 10000.0
MIX_WIDTH = CONV_CH + GDN_WIDTH + ATTN_WIDTH
N_GROUPS = 4
EXPERTS_PER_GROUP = 8
N_EXPERTS = N_GROUPS * EXPERTS_PER_GROUP
TOP_K = 2
D_EXPERT = 512
MOE_BLOCK = 128

IN_SIZES = (GDN_QKV, 2 * GDN_HEADS, 2 * GDN_HEADS,
            ATTN_KV_HEADS * HEAD_DIM, ATTN_KV_HEADS * HEAD_DIM,
            CONV_CH, CONV_CH, GDN_WIDTH, ATTN_WIDTH)
CTX_STATE_COLS = GDN_QKV + 4 * GDN_HEADS + 2 * ATTN_KV_HEADS * HEAD_DIM
D_IN = CTX_STATE_COLS + 2 * CONV_CH + GDN_WIDTH + ATTN_WIDTH

kernel_name = "hybrid_conv_deltanet_gqa_hmoe_dit"

def split_cols(t, sizes):
    out, off = [], 0
    for s in sizes:
        out.append(t[..., off:off + s])
        off += s
    return out

def rms_norm(x, g):
    xf = x.astype(jnp.float32)
    y = xf * lax.rsqrt(jnp.mean(xf * xf, axis=-1, keepdims=True) + EPS)
    return (y * g.astype(jnp.float32)).astype(x.dtype)

def layer_norm(x, g, b):
    xf = x.astype(jnp.float32)
    mu = jnp.mean(xf, axis=-1, keepdims=True)
    xc = xf - mu
    y = xc * lax.rsqrt(jnp.mean(xc * xc, axis=-1, keepdims=True) + EPS)
    return (y * g.astype(jnp.float32) + b.astype(jnp.float32)).astype(x.dtype)

def l2_norm(x):
    return x * lax.rsqrt(jnp.sum(x * x, axis=-1, keepdims=True) + EPS)

def depthwise_conv(x, w):
    pad = w.shape[0] // 2
    return lax.conv_general_dilated(
        x, w[:, None, :].astype(x.dtype), window_strides=(1,), padding=[(pad, pad)],
        dimension_numbers=("NWC", "WIO", "NWC"), feature_group_count=x.shape[-1])

def axial_rope_tables(n_tokens):
    rows = n_tokens // GRID_W
    row = jnp.repeat(jnp.arange(rows), GRID_W).astype(jnp.float32)
    col = (jnp.arange(rows * GRID_W) % GRID_W).astype(jnp.float32)
    n_freq = HEAD_DIM // 4
    inv = ROPE_THETA ** (-jnp.arange(n_freq, dtype=jnp.float32) / n_freq)
    ang = jnp.concatenate([row[:, None] * inv, col[:, None] * inv], axis=-1)
    return jnp.cos(ang), jnp.sin(ang)

def apply_axial_rope(x, cos, sin):
    L = x.shape[1]
    xr = x.astype(jnp.float32).reshape(*x.shape[:-1], 2, 2, HEAD_DIM // 4)
    x1, x2 = xr[..., 0, :], xr[..., 1, :]
    c = cos.reshape(L, 2, HEAD_DIM // 4)[None, :, None]
    s = sin.reshape(L, 2, HEAD_DIM // 4)[None, :, None]
    out = jnp.stack([x1 * c - x2 * s, x2 * c + x1 * s], axis=-2)
    return out.reshape(x.shape).astype(x.dtype)

def conformer_conv(val, gate, dw_w, dw_b, ln_g, ln_b, pw_w, pw_b):
    h = val * jax.nn.sigmoid(gate)
    h = depthwise_conv(h, dw_w) + dw_b
    h = jax.nn.silu(layer_norm(h, ln_g, ln_b))
    return h @ pw_w + pw_b

def gdn_features(qkv, a_in, b_in, conv_w, a_log, dt_bias):
    B, L, _ = qkv.shape
    qkv = jax.nn.silu(depthwise_conv(qkv, conv_w)).astype(jnp.float32)
    q, k, v = split_cols(qkv, (GDN_HEADS * GDN_DK, GDN_HEADS * GDN_DK, GDN_WIDTH))
    q = l2_norm(q.reshape(B, L, GDN_HEADS, GDN_DK)) * (GDN_DK ** -0.5)
    k = l2_norm(k.reshape(B, L, GDN_HEADS, GDN_DK))
    v = v.reshape(B, L, GDN_HEADS, GDN_DV)
    a_in = a_in.astype(jnp.float32).reshape(B, L, 2, GDN_HEADS)
    b_in = b_in.astype(jnp.float32).reshape(B, L, 2, GDN_HEADS)
    g = -jnp.exp(a_log.astype(jnp.float32)) * jax.nn.softplus(a_in + dt_bias.astype(jnp.float32))
    beta = jax.nn.sigmoid(b_in)
    return q, k, v, g, beta

def gdn_direction(q, k, v, g, beta, s0, with_out):
    B, L, H, _ = q.shape
    dv = v.shape[-1]
    n = L // GDN_CHUNK

    def chunks(t):
        return jnp.moveaxis(t.reshape(B, n, GDN_CHUNK, H, *t.shape[3:]), 3, 1)

    q, k, v, g, beta = (chunks(t) for t in (q, k, v, g, beta))
    gam = jnp.cumsum(g, axis=-1)
    idx = jnp.arange(GDN_CHUNK)
    incl = idx[:, None] >= idx[None, :]
    strict = idx[:, None] > idx[None, :]
    decay = jnp.exp(jnp.where(incl, gam[..., :, None] - gam[..., None, :], -jnp.inf))
    kb = k * beta[..., None]
    a = jnp.where(strict, jnp.einsum("bhncd,bhnsd->bhncs", kb, k) * decay, 0.0)
    rhs = jnp.concatenate([v * beta[..., None], kb * jnp.exp(gam)[..., None]], axis=-1)
    sol = lax.linalg.triangular_solve(a, rhs, left_side=True, lower=True, unit_diagonal=True)
    u, w = sol[..., :dv], sol[..., dv:]
    last = gam[..., -1]
    kd = k * jnp.exp(last[..., None] - gam)[..., None]
    xs = [u, w, kd, jnp.exp(last)]
    if with_out:
        p = jnp.einsum("bhncd,bhnsd->bhncs", q, k) * decay
        xs += [p, q * jnp.exp(gam)[..., None]]
    xs = tuple(jnp.moveaxis(t, 2, 0) for t in xs)

    def step(s, inp):
        u_n, w_n, kd_n, gl_n = inp[:4]
        v_new = u_n - jnp.einsum("bhck,bhkv->bhcv", w_n, s)
        s_new = s * gl_n[..., None, None] + jnp.einsum("bhck,bhcv->bhkv", kd_n, v_new)
        if with_out:
            p_n, qg_n = inp[4:]
            o = jnp.einsum("bhck,bhkv->bhcv", qg_n, s) + jnp.einsum("bhcs,bhsv->bhcv", p_n, v_new)
            return s_new, o
        return s_new, None

    s_fin, o = lax.scan(step, s0, xs)
    if not with_out:
        return None, s_fin
    o = jnp.transpose(o, (1, 0, 3, 2, 4)).reshape(B, L, H, dv)
    return o, s_fin

def gdn_bidirectional(feats_c, feats_l, with_ctx_out):
    qc, kc, vc, gc, bc = feats_c
    ql, kl, vl, gl, bl = feats_l
    B = ql.shape[0]
    s0 = jnp.zeros((B, GDN_HEADS, GDN_DK, GDN_DV), jnp.float32)
    o_lat, o_ctx = 0.0, 0.0
    for d in range(2):
        flip = (lambda t: jnp.flip(t, axis=1)) if d == 1 else (lambda t: t)
        oc, sc = gdn_direction(flip(qc), flip(kc), flip(vc), flip(gc[:, :, d]), flip(bc[:, :, d]), s0, with_ctx_out)
        ol, _ = gdn_direction(flip(ql), flip(kl), flip(vl), flip(gl[:, :, d]), flip(bl[:, :, d]), sc, True)
        o_lat = o_lat + flip(ol)
        if with_ctx_out:
            o_ctx = o_ctx + flip(oc)
    return o_lat, (o_ctx if with_ctx_out else None)

def gdn_output(o, z, norm_g, dtype):
    B, L = o.shape[:2]
    zf = z.astype(jnp.float32).reshape(B, L, GDN_HEADS, GDN_DV)
    y = rms_norm(o, norm_g) * jax.nn.silu(zf)
    return y.reshape(B, L, GDN_WIDTH).astype(dtype)

def attend(qb, keys, vals):
    s = jnp.einsum("bqkgd,bskd->bkgqs", qb, keys, preferred_element_type=jnp.float32) * (HEAD_DIM ** -0.5)
    p = jax.nn.softmax(s, axis=-1)
    return jnp.einsum("bkgqs,bskd->bqkgd", p.astype(vals.dtype), vals)

def gqa_attention(q_l, k_l, v_l, q_c, k_c, v_c, q_norm_g, k_norm_g, cos, sin):
    B, L, _ = q_l.shape
    Lc = k_c.shape[1]

    def heads(t, h):
        return t.reshape(t.shape[0], t.shape[1], h, HEAD_DIM)

    ql = apply_axial_rope(rms_norm(heads(q_l, ATTN_Q_HEADS), q_norm_g), cos, sin)
    kl = apply_axial_rope(rms_norm(heads(k_l, ATTN_KV_HEADS), k_norm_g), cos, sin)
    kc = rms_norm(heads(k_c, ATTN_KV_HEADS), k_norm_g)
    vc = heads(v_c, ATTN_KV_HEADS)
    keys = jnp.concatenate([kc, kl], axis=1)
    vals = jnp.concatenate([vc, heads(v_l, ATTN_KV_HEADS)], axis=1)
    nb = L // Q_BLOCK
    qb = ql.reshape(B, nb, Q_BLOCK, ATTN_KV_HEADS, ATTN_GROUP, HEAD_DIM).transpose(1, 0, 2, 3, 4, 5)
    ob = lax.map(lambda t: attend(t, keys, vals), qb)
    o_l = ob.transpose(1, 0, 2, 3, 4, 5).reshape(B, L, ATTN_WIDTH)
    if q_c is None:
        return o_l, None
    qc = rms_norm(heads(q_c, ATTN_Q_HEADS), q_norm_g).reshape(B, Lc, ATTN_KV_HEADS, ATTN_GROUP, HEAD_DIM)
    o_c = attend(qc, kc, vc).reshape(B, Lc, ATTN_WIDTH)
    return o_l, o_c

def hierarchical_moe(x, wr_g, br_g, wr_e, br_e, w_gate, w_up, w_down):
    T, D = x.shape
    xf = x.astype(jnp.float32)
    pg = jax.nn.softmax(xf @ wr_g.astype(jnp.float32) + br_g.astype(jnp.float32), axis=-1)
    grp = jnp.argmax(pg, axis=-1)
    pg_sel = jnp.take_along_axis(pg, grp[:, None], axis=-1)
    le = (xf @ wr_e.astype(jnp.float32) + br_e.astype(jnp.float32)).reshape(T, N_GROUPS, EXPERTS_PER_GROUP)
    le = jnp.take_along_axis(le, grp[:, None, None], axis=1)[:, 0]
    top_p, top_i = lax.top_k(jax.nn.softmax(le, axis=-1), TOP_K)
    wts = pg_sel * top_p / jnp.sum(top_p, axis=-1, keepdims=True)
    eid = grp[:, None] * EXPERTS_PER_GROUP + top_i
    flat_e = eid.reshape(-1)
    flat_t = jnp.repeat(jnp.arange(T, dtype=jnp.int32), TOP_K)
    flat_w = wts.reshape(-1)
    order = jnp.argsort(flat_e)
    se, st, sw = flat_e[order], flat_t[order], flat_w[order]
    counts = jnp.bincount(flat_e, length=N_EXPERTS)
    starts = jnp.cumsum(counts) - counts
    pcounts = (counts + MOE_BLOCK - 1) // MOE_BLOCK * MOE_BLOCK
    pends = jnp.cumsum(pcounts)
    pstarts = pends - pcounts
    slot = pstarts[se] + jnp.arange(T * TOP_K) - starts[se]
    n_slots = -(-(T * TOP_K) // MOE_BLOCK) * MOE_BLOCK + N_EXPERTS * MOE_BLOCK
    slot_tok = jnp.full((n_slots,), T, jnp.int32).at[slot].set(st)
    slot_w = jnp.zeros((n_slots,), x.dtype).at[slot].set(sw.astype(x.dtype))
    nblk = n_slots // MOE_BLOCK
    blk_e = jnp.minimum(jnp.searchsorted(pends, jnp.arange(nblk) * MOE_BLOCK, side="right"), N_EXPERTS - 1)
    xpad = jnp.concatenate([x, jnp.zeros((1, D), x.dtype)], axis=0)
    xb = xpad[slot_tok].reshape(nblk, MOE_BLOCK, D)

    def expert_block(args):
        xe, e = args
        h = jax.nn.silu(xe @ w_gate[e]) * (xe @ w_up[e])
        return h @ w_down[e]

    yb = lax.map(expert_block, (xb, blk_e)).reshape(n_slots, D)
    out = jnp.zeros_like(xpad).at[slot_tok].add(yb * slot_w[:, None])
    return out[:T]

def trunk_layer(x, ctx, c, c_ctx, cos, sin, with_ctx_out,
                mod_w, mod_b, norm1_g, norm2_g, w_in,
                conv_dw_w, conv_dw_b, conv_ln_g, conv_ln_b, conv_pw_w, conv_pw_b,
                gdn_conv_w, gdn_a_log, gdn_dt_bias, gdn_norm_g,
                attn_q_norm_g, attn_k_norm_g, w_out,
                router_group_w, router_group_b, router_expert_w, router_expert_b,
                expert_w_gate, expert_w_up, expert_w_down):
    B, L, D = x.shape
    Lc = ctx.shape[1]
    mod_l = (jax.nn.silu(c) @ mod_w + mod_b)[:, None, :]
    mod_c = (jax.nn.silu(c_ctx) @ mod_w + mod_b)[None, None, :]
    sh1_l, sc1_l, g1_l, sh2_l, sc2_l, g2_l = split_cols(mod_l, (D,) * 6)
    sh1_c, sc1_c, g1_c, sh2_c, sc2_c, g2_c = split_cols(mod_c, (D,) * 6)

    h_l = rms_norm(x, norm1_g) * (1 + sc1_l) + sh1_l
    h_c = rms_norm(ctx, norm1_g) * (1 + sc1_c) + sh1_c
    qkv_l, a_l, b_l, k_l, v_l, gv_l, gg_l, z_l, q_l = split_cols(h_l @ w_in, IN_SIZES)
    if with_ctx_out:
        qkv_c, a_c, b_c, k_c, v_c, gv_c, gg_c, z_c, q_c = split_cols(h_c @ w_in, IN_SIZES)
    else:
        qkv_c, a_c, b_c, k_c, v_c = split_cols(h_c @ w_in[:, :CTX_STATE_COLS], IN_SIZES[:5])
        q_c = None

    conv_args = (conv_dw_w, conv_dw_b, conv_ln_g, conv_ln_b, conv_pw_w, conv_pw_b)
    conv_out_l = conformer_conv(gv_l, gg_l, *conv_args)
    feats_c = gdn_features(qkv_c, a_c, b_c, gdn_conv_w, gdn_a_log, gdn_dt_bias)
    feats_l = gdn_features(qkv_l, a_l, b_l, gdn_conv_w, gdn_a_log, gdn_dt_bias)
    o_gdn_l, o_gdn_c = gdn_bidirectional(feats_c, feats_l, with_ctx_out)
    gdn_out_l = gdn_output(o_gdn_l, z_l, gdn_norm_g, x.dtype)
    attn_l, attn_c = gqa_attention(q_l, k_l, v_l, q_c, k_c, v_c, attn_q_norm_g, attn_k_norm_g, cos, sin)
    x = x + g1_l * (jnp.concatenate([conv_out_l, gdn_out_l, attn_l], axis=-1) @ w_out)
    if with_ctx_out:
        conv_out_c = conformer_conv(gv_c, gg_c, *conv_args)
        gdn_out_c = gdn_output(o_gdn_c, z_c, gdn_norm_g, ctx.dtype)
        ctx = ctx + g1_c * (jnp.concatenate([conv_out_c, gdn_out_c, attn_c], axis=-1) @ w_out)

    moe_args = (router_group_w, router_group_b, router_expert_w, router_expert_b,
                expert_w_gate, expert_w_up, expert_w_down)
    h2_l = (rms_norm(x, norm2_g) * (1 + sc2_l) + sh2_l).reshape(B * L, D)
    if with_ctx_out:
        h2_c = (rms_norm(ctx, norm2_g) * (1 + sc2_c) + sh2_c).reshape(B * Lc, D)
        y = hierarchical_moe(jnp.concatenate([h2_l, h2_c], axis=0), *moe_args)
        x = x + g2_l * y[:B * L].reshape(B, L, D)
        ctx = ctx + g2_c * y[B * L:].reshape(B, Lc, D)
        return x, ctx
    y = hierarchical_moe(h2_l, *moe_args)
    return x + g2_l * y.reshape(B, L, D), None

def setup_inputs(seed: int = 0) -> dict:
    key = jax.random.key(seed)
    ks = jax.random.split(key, 32)
    f32 = jnp.float32
    D = D_MODEL

    def nrm(k, shape, scale):
        return jax.random.normal(k, shape, f32) * scale

    def gain(k, shape):
        return 1.0 + 0.1 * jax.random.normal(k, shape, f32)

    dt = jnp.exp(jax.random.uniform(ks[17], (DEPTH, 2, GDN_HEADS), f32, math.log(1e-3), math.log(1e-1)))
    return {
        "x": nrm(ks[0], (BATCH, SEQ, D), 1.0),
        "c": nrm(ks[1], (BATCH, D), 1.0),
        "ctx": nrm(ks[2], (BATCH, CTX_LEN, D), 1.0),
        "c_ctx": nrm(ks[3], (D,), 1.0),
        "mod_w": nrm(ks[4], (DEPTH, D, 6 * D), 0.5 * D ** -0.5),
        "mod_b": nrm(ks[5], (DEPTH, 6 * D), 0.02),
        "norm1_g": gain(ks[6], (DEPTH, D)),
        "norm2_g": gain(ks[7], (DEPTH, D)),
        "w_in": nrm(ks[8], (DEPTH, D, D_IN), D ** -0.5),
        "conv_dw_w": nrm(ks[9], (DEPTH, CONV_WIDTH, CONV_CH), CONV_WIDTH ** -0.5),
        "conv_dw_b": nrm(ks[10], (DEPTH, CONV_CH), 0.02),
        "conv_ln_g": gain(ks[11], (DEPTH, CONV_CH)),
        "conv_ln_b": nrm(ks[12], (DEPTH, CONV_CH), 0.02),
        "conv_pw_w": nrm(ks[13], (DEPTH, CONV_CH, CONV_CH), CONV_CH ** -0.5),
        "conv_pw_b": nrm(ks[14], (DEPTH, CONV_CH), 0.02),
        "gdn_conv_w": nrm(ks[15], (DEPTH, SHORT_CONV, GDN_QKV), SHORT_CONV ** -0.5),
        "gdn_a_log": jnp.log(jax.random.uniform(ks[16], (DEPTH, 2, GDN_HEADS), f32, 1.0, 16.0)),
        "gdn_dt_bias": dt + jnp.log(-jnp.expm1(-dt)),
        "gdn_norm_g": gain(ks[18], (DEPTH, GDN_DV)),
        "attn_q_norm_g": gain(ks[19], (DEPTH, HEAD_DIM)),
        "attn_k_norm_g": gain(ks[20], (DEPTH, HEAD_DIM)),
        "w_out": nrm(ks[21], (DEPTH, MIX_WIDTH, D), MIX_WIDTH ** -0.5),
        "router_group_w": nrm(ks[22], (DEPTH, D, N_GROUPS), D ** -0.5),
        "router_group_b": nrm(ks[23], (DEPTH, N_GROUPS), 0.01),
        "router_expert_w": nrm(ks[24], (DEPTH, D, N_EXPERTS), D ** -0.5),
        "router_expert_b": nrm(ks[25], (DEPTH, N_EXPERTS), 0.01),
        "expert_w_gate": nrm(ks[26], (DEPTH, N_EXPERTS, D, D_EXPERT), D ** -0.5),
        "expert_w_up": nrm(ks[27], (DEPTH, N_EXPERTS, D, D_EXPERT), D ** -0.5),
        "expert_w_down": nrm(ks[28], (DEPTH, N_EXPERTS, D_EXPERT, D), D_EXPERT ** -0.5),
        "final_norm_g": gain(ks[29], (D,)),
    }

def reference(x, c, ctx, c_ctx, mod_w, mod_b, norm1_g, norm2_g, w_in,
              conv_dw_w, conv_dw_b, conv_ln_g, conv_ln_b, conv_pw_w, conv_pw_b,
              gdn_conv_w, gdn_a_log, gdn_dt_bias, gdn_norm_g,
              attn_q_norm_g, attn_k_norm_g, w_out,
              router_group_w, router_group_b, router_expert_w, router_expert_b,
              expert_w_gate, expert_w_up, expert_w_down, final_norm_g):
    cos, sin = axial_rope_tables(x.shape[1])
    for layer in range(DEPTH):
        x, ctx = trunk_layer(
            x, ctx, c, c_ctx, cos, sin, layer < DEPTH - 1,
            mod_w[layer], mod_b[layer], norm1_g[layer], norm2_g[layer], w_in[layer],
            conv_dw_w[layer], conv_dw_b[layer], conv_ln_g[layer], conv_ln_b[layer],
            conv_pw_w[layer], conv_pw_b[layer],
            gdn_conv_w[layer], gdn_a_log[layer], gdn_dt_bias[layer], gdn_norm_g[layer],
            attn_q_norm_g[layer], attn_k_norm_g[layer], w_out[layer],
            router_group_w[layer], router_group_b[layer], router_expert_w[layer], router_expert_b[layer],
            expert_w_gate[layer], expert_w_up[layer], expert_w_down[layer])
    return rms_norm(x, final_norm_g)


_drawn_inputs = setup_inputs


def setup_inputs(seed=0):
    import zlib

    import numpy as np

    out = dict(_drawn_inputs(seed))
    spreads = {}
    factors = {'ctx': 5.496,
     'c_ctx': 3.426,
     'mod_b': 2.77,
     'conv_dw_b': 8.0,
     'conv_ln_g': 4.074,
     'conv_ln_b': 26.865,
     'conv_pw_b': 7.938,
     'gdn_dt_bias': 2.854,
     'gdn_norm_g': 4.497,
     'attn_q_norm_g': 8.0,
     'attn_k_norm_g': 8.0,
     'router_group_b': 49.406,
     'router_expert_b': 33.249}
    for name, (base, spread) in spreads.items():
        noise = np.random.default_rng([zlib.crc32(name.encode()), seed]).standard_normal(out[name].shape)
        drawn = base * np.exp(spread * noise) if base else spread * noise
        out[name] = jnp.asarray(drawn.astype(out[name].dtype))
    for name, factor in factors.items():
        out[name] = (out[name] * factor).astype(out[name].dtype)
    return out
```

```python
from contextlib import ExitStack

import concourse.bass as bass
from concourse import mybir

F32 = mybir.dt.float32
F32R = mybir.dt.float32r
I32 = mybir.dt.int32
U32 = mybir.dt.uint32
ALU = mybir.AluOpType
ACT = mybir.ActivationFunctionType
AX = mybir.AxisListType

P = 128
D = 1024
KT = D // P
L, LC = 1024, 256
NT, NCT = L // P, LC // P
TA = NT + NCT
TOK = L + LC
EPS = 1e-6
NH, HD = 4, 64
QH, KVH = 8, 2
CW, SW = 31, 5
NE, NG, EPG, FE = 32, 4, 8, 512
NEG = -1e30

C_QKV, C_AB, C_KV, C_GV, C_GG, C_Z, C_Q = 0, 768, 784, 1040, 1296, 1552, 1808
D_IN = 2320


def constants():
    import numpy as np
    p, f = np.arange(P)[:, None], np.arange(P)[None, :]
    same = p // 64 == f // 64
    fwd = [same & (f < p), same & (f >= p)]
    bwd = [same & (f > p), same & (f <= p)]
    mats = [(p == f)]
    for strict, incl in (fwd, bwd):
        mats += [incl]
    adds = [np.where(m, 0.0, NEG) for m in (fwd[0], bwd[0], fwd[1], bwd[1])]
    levels = []
    for d in range(2):
        for s in (1, 2, 4, 8, 16, 32):
            a, b = (p, f) if d == 0 else (f, p)
            levels.append((a // (2 * s) == b // (2 * s)) & (a // s % 2 == 1) & (b // s % 2 == 0))
    mats = mats + levels
    earlier = p < f
    cst = np.concatenate([np.asarray(m, np.float32) for m in mats + adds + [earlier]], axis=1)
    row = np.repeat(np.arange(L // 64), 64).astype(np.float32)
    col = (np.arange(L) % 64).astype(np.float32)
    inv = (10000.0 ** (-np.arange(16, dtype=np.float32) / 16)).astype(np.float32)
    ang = np.stack([row[:, None] * inv, col[:, None] * inv], axis=1)
    cos = np.cos(ang).astype(np.float32)
    sin = np.sin(ang).astype(np.float32)
    ctab = np.stack([cos, cos], axis=2).reshape(L, 64)
    stab = np.stack([-sin, sin], axis=2).reshape(L, 64)
    rope = np.concatenate([ctab, stab], axis=1).astype(np.float32)
    return cst, rope


M_ID, M_PRE, M_LEV, M_STRICT, M_INCL, M_EARLY = 0, 1, 3, 15, 17, 19
N_CST = 20


def trunk(nc, x, c, ctx_in, c_ctx, mod_w, mod_b, norm1_g, norm2_g, w_in,
          conv_dw_w, conv_dw_b, conv_ln_g, conv_ln_b, conv_pw_w, conv_pw_b,
          gdn_conv_w, gdn_a_log, gdn_dt_bias, gdn_norm_g, attn_q_norm_g, attn_k_norm_g, w_out,
          router_group_w, router_group_b, router_expert_w, router_expert_b,
          expert_w_gate, expert_w_up, expert_w_down, final_norm_g, cst, rope, out):
    ctx = ExitStack()
    with ctx:
        live = []

        def sem(name):
            live.append(nc.alloc_semaphore(name))
            return live[-1]

        def retire_semaphores():
            nc.clear_and_free_semaphores(live)
            nc.all_engine_barrier()
            live.clear()

        ARENA = (nc.sbuf_base + 31) // 32 * 32
        CUT, ALL = 49788, 53000
        arena = ctx.enter_context(nc.sbuf_tensor("arena", [P, CUT], F32))
        small = ctx.enter_context(nc.sbuf_tensor("small", [P, ALL - CUT], F32))
        psum = ctx.enter_context(nc.psum_tensor("psum", [P, 8, 512], F32))

        def at(kb, *dims, dt=F32):
            n = 1
            for d in dims:
                n *= d
            o = int(kb * 256)
            v = arena[:, o:o + n] if o < CUT else small[:, o - CUT:o - CUT + n]
            if dt != F32:
                v = v.bitcast(dt)
            if len(dims) == 2:
                v = v.rearrange("p (a b) -> p a b", a=dims[0])
            elif len(dims) == 3:
                v = v.rearrange("p (a b c) -> p a b c", a=dims[0], b=dims[1])
            elif len(dims) == 4:
                v = v.rearrange("p (a b c d) -> p a b c d", a=dims[0], b=dims[1], c=dims[2])
            return v

        def at_r(name, kb, *dims):
            n = 1
            for d in dims:
                n *= d
            v = nc.alloc_sbuf_tensor_at(name, [P, n], F32R, offset=ARENA + int(kb * 1024))[:]
            if len(dims) == 2:
                v = v.rearrange("p (a b) -> p a b", a=dims[0])
            elif len(dims) == 3:
                v = v.rearrange("p (a b c) -> p a b c", a=dims[0], b=dims[1])
            elif len(dims) == 4:
                v = v.rearrange("p (a b c d) -> p a b c d", a=dims[0], b=dims[1], c=dims[2])
            return v

        def drow(v, n=P):
            return v.flatten().partition_broadcast(n)

        hT = at(0, KT, TOK)
        w12 = at(40, KT, C_Z)
        ring = at(90, 3, 2048)
        w3 = at(90, KT, D_IN - C_Z)
        modrow, modb = at(115, 2048), at(123, 2048)
        xin = at(131, 6, D)
        qkvT = at(155, 6, 1288)
        cvg = at(186.25, 2, L + CW - 1)
        abT = at(194.75, TOK)
        kvtok = at(131, TA, 256)
        qtok = at(115, NT, QH * HD)
        zs = at(141, NT, 256)
        ident = at(199.75, P)
        o = 200.25
        cT, cS = at(o, 2, KT), at(o + .0625, 2, KT)
        n1g, n2g = at(o + .125, KT), at(o + .15625, KT)
        colA1, colB1 = at(o + .1875, KT, 2), at(o + .25, KT, 2)
        colA2, colB2 = at(o + .3125, KT), at(o + .34375, KT)
        ssq, rstd = at(o + .375, 16), at(o + .4375, 16)
        epst = at(o + .5, 1)

        NB = 48
        NB_MIN = L * 2 // P + 1
        y_dram = nc.dram_tensor("expert_out", (NB * P, D), F32).ap()
        gate_dram = nc.dram_tensor("gate_rows", (2, D), F32).ap()

        s_small, s_id = sem("s_small"), sem("s_id")
        s_x = [sem(f"s_x{i}") for i in range(6)]
        s_w12, s_w12b, s_w3, s_modb = sem("s_w12"), sem("s_w12b"), sem("s_w3"), sem("s_modb")
        s_ring = [sem(f"s_ring{i}") for i in range(3)]
        s_pads, s_cs = sem("s_pads"), sem("s_cs")
        s_slice, s_modrow, s_cols, s_colv = sem("s_slice"), sem("s_modrow"), sem("s_cols"), sem("s_colv")
        s_gates = sem("s_gates")
        s_ssq, s_std, s_rstd, s_xn = sem("s_ssq"), sem("s_std"), sem("s_rstd"), sem("s_xn")
        s_pj, s_pja, s_pjd = sem("s_pj"), sem("s_pja"), sem("s_pjd")
        s_dl, s_al, s_pl = sem("s_dl"), sem("s_al"), sem("s_pl")

        GROUPS = [(0, 2), (2, 4), (6, 4)]
        CHUNKS = [(0, 256), (256, 512), (768, 512)]
        jobs = [("xT", g, k, "AD"[k % 2]) for g in range(3) for k in range(KT)]
        jobs += [("qkv", m, ch, "AD"[(m * 3 + ch) % 2]) for m in range(6) for ch in range(3)]
        for m in range(2):
            for ch in (1, 2):
                jobs += [("gg", m, ch, "A"), ("gv", m, ch, "D")]
        jobs += [("ab", 0, ch, "A") for ch in range(3)]
        jobs += [("kv", t, 0, "AD"[t % 2]) for t in range(TA)]
        for t in range(NT):
            jobs += [("z", t, 0, "A"), ("q", t, 0, "D")]
        NJ = len(jobs)

        def evacuated(n, e):
            return sum(j[3] == e for j in jobs[:n + 1])

        def jbank(n):
            return psum[:, 4 + n % 4, :]

        SLICES = 3 * KT
        MOD_AT = {s: 24 + (s - 8) for s in range(8, SLICES)}
        MOD_SLICE = {n: s for s, n in MOD_AT.items()}
        sig = at(149, 2, 512)

        def job_ready(eng, n):
            if n >= 4:
                e = jobs[n - 4][3]
                eng.wait_ge(s_pja if e == "A" else s_pjd, evacuated(n - 4, e))

        def evac_jobs(eng, me, n0, n1):
            for n in range(n0, n1):
                kind, i, j, e = jobs[n]
                if e != me:
                    continue
                if n == 0 or n == 1:
                    eng.wait_ge(s_colv, 2)
                    if me == "A":
                        eng.wait_ge(s_pads, 1)
                eng.wait_ge(s_pj, n + 1)
                b = jbank(n)
                done = s_pja if e == "A" else s_pjd
                if kind == "xT":
                    a0, na = GROUPS[i]
                    w = 1 if i == 0 else 0
                    dst, src = hT[:, j, a0 * P:(a0 + na) * P], b[:, 0:na * P]
                    if e == "A":
                        nc.scalar.activation(dst, src, ACT.Identity, bias=colB1[:, j, w:w + 1],
                                             scale=colA1[:, j, w:w + 1]).then_inc(done, 1)
                    else:
                        nc.vector.tensor_scalar(dst, src, colA1[:, j, w:w + 1], colB1[:, j, w:w + 1],
                                                ALU.mult, ALU.add).then_inc(done, 1)
                    continue
                if kind == "gg":
                    if n >= 46:
                        eng.wait_ge(s_pjd, evacuated(n - 3, "D"))
                    nc.scalar.activation(sig[:, n // 2 % 2], b, ACT.Sigmoid).then_inc(done, 1)
                    continue
                if kind == "gv":
                    eng.wait_ge(s_pja, evacuated(n - 1, "A"))
                    t0 = 15 + CHUNKS[j][0] - LC
                    nc.vector.tensor_tensor(cvg[:, i, t0:t0 + 512], b, sig[:, n // 2 % 2], ALU.mult).then_inc(done, 1)
                    continue
                if kind == "qkv":
                    t0, nt = CHUNKS[j]
                    o = 2 + t0 + (4 if j else 0)
                    dst, src = qkvT[:, i, o:o + nt], b[:, 0:nt]
                elif kind == "ab":
                    t0, nt = CHUNKS[j]
                    dst, src = abT[0:16, t0:t0 + nt], b[0:16, 0:nt]
                elif kind == "kv":
                    dst, src = kvtok[:, i, :], b[:, 0:256]
                elif kind == "z":
                    nc.scalar.activation(zs[:, i, :], b[:, 0:256], ACT.Silu).then_inc(done, 1)
                    continue
                elif kind == "q":
                    if i == 0:
                        eng.wait_ge(s_gates, 32)
                        eng.wait_ge(s_cols, 3)
                    dst, src = qtok[:, i, :], b
                if e == "A":
                    nc.scalar.activation(dst, src, ACT.Copy).then_inc(done, 1)
                else:
                    nc.vector.tensor_copy(dst, src).then_inc(done, 1)

        front = ExitStack()
        block = front.enter_context(nc.Block())

        @block.sync
        def _(sp):
            sp.dma_start(ident, cst[:, 0:P]).then_inc(s_id, 16)
            sp.dma_start(cT[:, 0, :], c.rearrange("a (p k) -> p (a k)", k=KT)).then_inc(s_small, 16)
            sp.dma_start(cT[:, 1, :], c_ctx.rearrange("(p k) -> p k", k=KT)).then_inc(s_small, 16)
            sp.dma_start(n1g, norm1_g.rearrange("a (k p) -> p (a k)", p=P), allow_slow_non_contiguous=True).then_inc(s_small, 16)
            sp.dma_start(n2g, norm2_g.rearrange("a (k p) -> p (a k)", p=P), allow_slow_non_contiguous=True).then_inc(s_small, 16)
            mw = mod_w.rearrange("a (p k) n -> p (a k) n", k=KT)

            def slice_in(s):
                g, kt = divmod(s, KT)
                if s >= 3:
                    sp.wait_ge(s_slice, s - 2)
                sp.dma_start(ring[:, s % 3, :], mw[:, kt, g * 2048:(g + 1) * 2048]).then_inc(s_ring[s % 3], 16)

            def bias_in(g):
                if g:
                    sp.wait_ge(s_modrow, g)
                sp.dma_start(modb[0:2, :], drow(mod_b[0:1, g * 2048:(g + 1) * 2048], 2)).then_inc(s_modb, 16)

            def x_in(a):
                src = ctx_in[0, a * P:(a + 1) * P, :] if a < NCT else x[0, (a - NCT) * P:(a - NCT + 1) * P, :]
                if a >= 6:
                    sp.wait_ge(s_pj, KT if a < 8 else 2 * KT)
                sp.dma_start(xin[:, a % 6, :], src).then_inc(s_x[a % 6], 16)

            bias_in(0)
            for s in range(3):
                slice_in(s)
                x_in(s)
            for s in range(3, 8):
                slice_in(s)
                if s < 6:
                    x_in(s)
            wv = w_in.rearrange("a (k p) n -> p (a k) n", p=P)
            sp.dma_start(w12[:, :, 0:C_KV], wv[:, :, 0:C_KV]).then_inc(s_w12, 16)
            for a in (6, 7, 8, 9):
                x_in(a)
            sp.dma_start(w12[:, :, C_KV:C_Z], wv[:, :, C_KV:C_Z]).then_inc(s_w12b, 16)
            bias_in(1)
            for s in range(8, SLICES):
                slice_in(s)
                if s == 17:
                    bias_in(2)
                    sp.dma_start(gate_dram[0:1, :], modrow[0:1, 0:D]).then_inc(s_gates, 16)
            sp.wait_ge(s_slice, SLICES)
            sp.dma_start(w3, wv[:, :, C_Z:D_IN]).then_inc(s_w3, 16)
            sp.wait_ge(s_modrow, 3)
            sp.dma_start(gate_dram[1:2, :], modrow[0:1, D:2 * D]).then_inc(s_gates, 16)

        @block.gpsimd
        def _(pool):
            for v in (qkvT[:, :, 0:2], qkvT[:, :, 258:262], qkvT[:, :, 1286:1288],
                      cvg[:, :, 0:15], cvg[:, :, 15 + L:30 + L]):
                last = nc.gpsimd.memset(v, 0.0)
            last = nc.gpsimd.memset(epst, EPS)
            last.then_inc(s_pads, 1)
        @block.scalar
        def _(act):
            act.wait_ge(s_small, 64)
            act.wait_ge(s_pads, 1)
            nc.scalar.activation(cS, cT, ACT.Silu).then_inc(s_cs, 1)
            for a in range(TA):
                act.wait_ge(s_x[a % 6], 16 * (a // 6 + 1))
                if a:
                    act.wait_ge(s_ssq, a)
                nc.scalar.activation(at(194.75, D), xin[:, a % 6, :], ACT.Square,
                                     accum_out=ssq[:, a:a + 1]).then_inc(s_ssq, 1)
                if a in (1, 5, 9):
                    g = a // 4
                    a0, na = GROUPS[g]
                    act.wait_ge(s_ssq, a0 + na)
                    nc.scalar.activation(rstd[:, a0:a0 + na], ssq[:, a0:a0 + na], ACT.Sqrt, bias=epst,
                                         scale=1.0 / D).then_inc(s_std, 1)
                if a in (5, 7):
                    evac_jobs(act, "A", KT * (a == 7), KT * (a == 7) + KT)
            evac_jobs(act, "A", 16, NJ)

        @block.vector
        def _(dve):
            def mod_rows(g):
                dve.wait_ge(s_slice, 8 * (g + 1))
                dve.wait_ge(s_modb, 16 * (g + 1))
                if g:
                    dve.wait_ge(s_cols, g)
                if g == 2:
                    dve.wait_ge(s_gates, 16)
                for j in range(4):
                    last = nc.vector.tensor_tensor(modrow[0:2, j * 512:(j + 1) * 512],
                                                   psum[32 * j:32 * j + 2, g, :],
                                                   modb[0:2, j * 512:(j + 1) * 512], ALU.add)
                last.then_inc(s_modrow, 1)

            def mod_cols(g):
                dve.wait_ge(s_cols, g + 1)
                dve.wait_ge(s_small, 64)
                v = psum[:, 3, 0:32].rearrange("p (h k w) -> p h k w", h=2, w=2)
                if g == 0:
                    nc.vector.tensor_copy(colB1, v[:, 0]).then_inc(s_colv, 1)
                    nc.vector.scalar_tensor_tensor(colA1, v[:, 1], 1.0, n1g.unsqueeze(2).broadcast_to([P, KT, 2]),
                                                   ALU.add, ALU.mult).then_inc(s_colv, 1)
                if g == 1:
                    nc.vector.tensor_copy(colB2, v[:, 1, :, 0]).then_inc(s_colv, 1)
                if g == 2:
                    nc.vector.scalar_tensor_tensor(colA2, v[:, 0, :, 0], 1.0, n2g,
                                                   ALU.add, ALU.mult).then_inc(s_colv, 1)

            mod_rows(0)
            mod_cols(0)
            dve.wait_ge(s_colv, 2)
            dve.wait_ge(s_pads, 1)
            for g, (a0, na) in enumerate(GROUPS):
                dve.wait_ge(s_std, g + 1)
                nc.vector.reciprocal(rstd[:, a0:a0 + na], rstd[:, a0:a0 + na]).then_inc(s_rstd, 1)
                dve.wait_ge(s_rstd, g + 1)
                for a in range(a0, a0 + na):
                    dve.wait_ge(s_x[a % 6], 16 * (a // 6 + 1))
                    nc.vector.tensor_scalar(xin[:, a % 6, :], xin[:, a % 6, :], rstd[:, a:a + 1], None,
                                            ALU.mult).then_inc(s_xn, 1)
                evac_jobs(dve, "D", 8 * g, 8 * g + 8)
            n1, n2 = MOD_AT[15], MOD_AT[23]
            evac_jobs(dve, "D", 24, n1 + 1)
            mod_rows(1)
            evac_jobs(dve, "D", n1 + 1, n1 + 3)
            mod_cols(1)
            evac_jobs(dve, "D", n1 + 3, n2 + 1)
            mod_rows(2)
            evac_jobs(dve, "D", n2 + 1, n2 + 3)
            mod_cols(2)
            evac_jobs(dve, "D", n2 + 3, NJ)

        @block.tensor
        def _(pe):
            def mod_slice(s):
                g, kt = divmod(s, KT)
                pe.wait_ge(s_ring[s % 3], 16 * (s // 3 + 1))
                for j in range(4):
                    last = nc.tensor.matmul(psum[32 * j:32 * j + 2, g, :], cS[:, :, kt],
                                            ring[:, s % 3, j * 512:(j + 1) * 512],
                                            start=kt == 0, stop=kt == KT - 1)
                last.then_inc(s_slice, 1)

            def mod_columns(g):
                pe.wait_ge(s_modrow, g + 1)
                if g:
                    pe.wait_ge(s_colv, g + 1)
                for h in {0: (0, 1), 1: (1,), 2: (0,)}[g]:
                    for k in range(KT):
                        c0 = h * D + k * P
                        o = (h * KT + k) * 2
                        last = nc.tensor.matmul(psum[:, 3, o:o + 2], modrow[0:2, c0:c0 + P], ident[0:2, 0:2],
                                                start=True, stop=True)
                last.then_inc(s_cols, 1)

            pe.wait_ge(s_cs, 1)
            pe.wait_ge(s_id, 16)
            for s in range(8):
                mod_slice(s)
            mod_columns(0)
            for n, (kind, i, j, e) in enumerate(jobs):
                job_ready(pe, n)
                b = jbank(n)
                if kind == "xT":
                    a0, na = GROUPS[i]
                    pe.wait_ge(s_xn, a0 + na)
                    for a in range(a0, a0 + na):
                        last = nc.tensor.transpose(b[:, (a - a0) * P:(a - a0 + 1) * P],
                                                   xin[:, a % 6, j * P:(j + 1) * P], ident)
                else:
                    if n == 24:
                        pe.wait_ge(s_w12, 16)
                        pe.wait_ge(s_pja, evacuated(23, "A"))
                        pe.wait_ge(s_pjd, evacuated(23, "D"))
                    if kind == "gg" and n == 42:
                        pe.wait_ge(s_w12b, 16)
                    if kind == "z" and i == 0:
                        pe.wait_ge(s_w3, 16)
                    for k in range(KT):
                        flags = dict(start=k == 0, stop=k == KT - 1)
                        if kind in ("qkv", "gg", "gv", "ab"):
                            c0 = {"qkv": C_QKV, "gg": C_GG, "gv": C_GV, "ab": C_AB}[kind] + i * P
                            m = 16 if kind == "ab" else P
                            t0, nt = CHUNKS[j]
                            last = nc.tensor.matmul(b[0:m, 0:nt], w12[:, k, c0:c0 + m], hT[:, k, t0:t0 + nt], **flags)
                        elif kind == "kv":
                            last = nc.tensor.matmul(b[:, 0:256], hT[:, k, i * P:(i + 1) * P],
                                                    w12[:, k, C_KV:C_KV + 256], **flags)
                        else:
                            c0, m = (0, 256) if kind == "z" else (256, 512)
                            a = NCT + i
                            last = nc.tensor.matmul(b[:, 0:m], hT[:, k, a * P:(a + 1) * P], w3[:, k, c0:c0 + m], **flags)
                last.then_inc(s_pj, 1)
                if n in MOD_SLICE:
                    s = MOD_SLICE[n]
                    mod_slice(s)
                if n in (MOD_AT[15] + 2, MOD_AT[23] + 2):
                    mod_columns(1 if n == MOD_AT[15] + 2 else 2)

        front.close()

        qn = at(0, NT, QH, HD)
        idr = at_r("ident_r", 16, P)
        attnT, convT = at(17, 4, L), at(33, 2, L)
        tmpq = at(41, NT, QH, HD)
        kn = at(57, TA, KVH, HD)
        k_hh = [at_r(f"k_hh{v}", 17 + 5 * v, TA, P) for v in range(KVH)]
        k_lo = [at_r(f"k_lo{v}", 27 + 5 * v, TA, P) for v in range(KVH)]
        zero_one = at(154.625, 2)
        kTh = at_r("kTh", 62.5, KVH, TOK)
        kTl = at_r("kTl", 72.5, KVH, TOK)
        vaug = at(82.5, TA, KVH, 3, HD)
        pT = at(97.5, 4, 512)
        q_hl = [at_r("q_hl0", 47, 4, P), at_r("q_hl1", 57, 4, P)]
        qT2 = at_r("qT2", 41, 3, 512)
        qTm = at_r("qTm", 105.5, 3, 512)
        ssh, rsh = at(113.5, 96), at(114, 96)
        sacc = at(115, 2, 1284)
        cacc = at(125.25, 2, L)
        ropet = at(149, NT, P)
        qgr, kgr = at(153, HD), at(153.25, HD)
        wtap_r = at(37, 1024)
        dwT, gwT = at(153.5625, 2, CW), at(154.125, 6, SW)
        ccol = at(154.25, 4, 2)
        pmax = at(154.3125, 4, 4, 3)
        nmax = at(154.5, 4, 4)
        eps64 = at(154.5625, 2)
        xtok = at(41, NT, 256)
        hcT = at(49, 2, L)
        wpw = at(57, 2, 256)
        stats = at(59, NT, 8)
        mv = at(59.25, NT, 2)
        lrs = at(59.5, NT)

        s2_rope, s2_gain, s2_tap, s2_col, s2_pw = (sem("s2_" + n) for n in ("rope", "gain", "tap", "col", "pw"))
        s2_zero, s2_vaug, s2_ssk, s2_ssq, s2_sq1 = (sem("s2_" + n) for n in ("zero", "vaug", "ssk", "ssq", "sq1"))
        s2_stdk, s2_stdq, s2_std1 = (sem("s2_" + n) for n in ("stdk", "stdq", "std1"))
        s2_k, s2_q0, s2_q1, s2_kt, s2_ktv = (sem("s2_" + n) for n in ("k", "q0", "q1", "kt", "ktv"))
        s2_v, s2_p, s2_rec1 = sem("s2_v"), sem("s2_p"), sem("s2_rec1")
        s2_tapt, s2_tapv = sem("s2_tapt"), sem("s2_tapv")
        s2_t, s2_qt, s2_a, s2_am, s2_nm, s2_row, s2_rowv = (
            sem("s2_" + n) for n in ("t", "qt", "a", "am", "nm", "row", "rowv"))
        s2_kn, s2_hi, s2_qs = (sem("s2_" + n) for n in ("kn", "hi", "qs"))
        s2_hi2, s2_qs2, s2_mul = sem("s2_hi2"), sem("s2_qs2"), sem("s2_mul")
        s2_zo, s2_qz = sem("s2_zo"), sem("s2_qz")
        tapped = at(49, 1284)
        s2_st, s2_exp, s2_pv, s2_rec, s2_o = (sem("s2_" + n) for n in ("st", "exp", "pv", "rec", "o"))
        s2_conv, s2_sconv, s2_back, s2_silu = (sem("s2_" + n) for n in ("conv", "sconv", "back", "silu"))
        s2_ct, s2_bn, s2_lstd, s2_ln, s2_hT, s2_hc, s2_pwm, s2_out = (
            sem("s2_" + n) for n in ("ct", "bn", "lstd", "ln", "hT", "hc", "pwm", "out"))

        SPLIT_DVE = 4
        JOBS = 2 * QH
        KTL = TA
        A_ITEMS = [(t, ch) for t in range(4) for ch in range(3)]
        KCH = [(0, 512), (512, 512), (1024, 256)]

        def bump(eng, s, ins, n):
            ins.then_inc(s, 1)
            eng.wait_ge(s, n)

        def norm_rope(eng, e, s, n, src, tmp, r, gain, dst, tiles, heads, lat0):
            rb = r.rearrange("p (t h) -> p t h", h=heads).unsqueeze(3).broadcast_to([P, tiles, heads, HD])
            gb = gain.unsqueeze(1).unsqueeze(1).broadcast_to([P, tiles, heads, HD])
            bump(eng, s, e.tensor_tensor(src, src, rb, ALU.mult), n + 1)
            bump(eng, s, e.tensor_tensor(src, src, gb, ALU.mult), n + 2)
            return n + 2

        def rotate(eng, e, s, n, src, tmp, dst, tile0, tiles, heads):
            for t in range(tiles):
                tab = ropet[:, tile0 + t, :]
                cb = tab[:, 0:64].unsqueeze(1).broadcast_to([P, heads, HD])
                e.tensor_tensor(dst[:, t], src[:, t], cb, ALU.mult)
                for hf in range(2):
                    o1 = tmp[:, t].rearrange("p h (a b c) -> p h a b c", a=2, b=2)[:, :, :, hf, :]
                    i1 = src[:, t].rearrange("p h (a b c) -> p h a b c", a=2, b=2)[:, :, :, 1 - hf, :]
                    sb_ = tab[:, 64:128].rearrange("p (a b c) -> p a b c", a=2, b=2)[:, :, hf, :]
                    last = e.tensor_tensor(o1, i1, sb_.unsqueeze(1).broadcast_to([P, heads, 2, 16]), ALU.mult)
            bump(eng, s, last, n + 1)
            return e.tensor_tensor(dst, dst, tmp, ALU.add)

        middle = ExitStack()
        b2 = middle.enter_context(nc.Block())

        conf_ops = [(m, j) for j in range(CW) for m in range(2)]
        short_ops = [(m0 + m, j) for m0 in (0, 2, 4) for j in range(SW) for m in range(2)]

        def split_queries(eng, e, n, hi, split, before_):
            hh, h = divmod(n, QH)
            src, dst = qn[:, hh * 4:hh * 4 + 4, h, :], q_hl[n % 2]
            if n >= 2:
                eng.wait_ge(s2_t, n - 1)
            e.tensor_copy(dst[:, :, 0:64], src).then_inc(hi, 1)
            eng.wait_ge(hi, before_ + 1)
            e.tensor_tensor(dst[:, :, 64:128], src, dst[:, :, 0:64], ALU.subtract).then_inc(split, 1)

        def short_step(pool, n):
            m, j = short_ops[n]
            if n == 0:
                pool.wait_ge(s2_tapv, 1)
            if n:
                pool.wait_ge(s2_sconv, n)
            if j == 0:
                if m >= 2:
                    pool.wait_ge(s2_back, m - 1)
                ins = nc.gpsimd.tensor_scalar(sacc[:, m % 2, :], qkvT[:, m, 0:1284], gwT[:, m, 0:1], None, ALU.mult)
            else:
                nc.gpsimd.tensor_scalar(tapped, qkvT[:, m, j:j + 1284], gwT[:, m, j:j + 1], None, ALU.mult
                                        ).then_inc(s2_mul, 1)
                pool.wait_ge(s2_mul, n // 10 * 8 + n % 10 - 1)
                ins = nc.gpsimd.tensor_tensor(sacc[:, m % 2, :], sacc[:, m % 2, :], tapped, ALU.add)
            ins.then_inc(s2_sconv, 1)

        @b2.sync
        def _(sp):
            sp.dma_start(ropet, rope.rearrange("(t p) n -> p t n", p=P)).then_inc(s2_rope, 16)
            sp.dma_start(qgr, drow(attn_q_norm_g)).then_inc(s2_gain, 16)
            sp.dma_start(kgr, drow(attn_k_norm_g)).then_inc(s2_gain, 16)
            sp.dma_start(wtap_r[0:CW, 0:256], conv_dw_w[0]).then_inc(s2_tap, 16)
            sp.dma_start(wtap_r[0:SW, 256:1024], gdn_conv_w[0]).then_inc(s2_tap, 16)
            for n, v in enumerate((conv_dw_b, conv_ln_g, conv_ln_b, conv_pw_b)):
                sp.dma_start(ccol[:, n, :], v.rearrange("a (m p) -> p (a m)", p=P),
                             allow_slow_non_contiguous=True).then_inc(s2_col, 16)
            sp.wait_ge(s2_pv, JOBS * KTL)
            sp.dma_start(wpw, conv_pw_w.rearrange("a (k p) n -> p (a k) n", p=P)).then_inc(s2_pw, 16)

        @b2.gpsimd
        def _(pool):
            nc.gpsimd.memset(eps64[:, 1:2], 64 * EPS)
            nc.gpsimd.memset(eps64[:, 0:1], EPS)
            nc.gpsimd.memset(zero_one[:, 0:1], 0.0)
            nc.gpsimd.memset(zero_one[:, 1:2], 1.0).then_inc(s2_zo, 1)
            pool.wait_ge(s2_zo, 1)
            for v in range(KVH):
                nc.gpsimd.tensor_copy(k_lo[v][:, :, 65:P], zero_one[:, 0:1].unsqueeze(1).broadcast_to([P, TA, 63]))
                nc.gpsimd.tensor_copy(k_lo[v][:, :, 64:65], zero_one[:, 1:2].unsqueeze(1).broadcast_to([P, TA, 1]))
            nc.gpsimd.tensor_copy(idr, ident)
            nc.gpsimd.memset(vaug[:, :, :, 0, :], 1.0)
            nc.gpsimd.memset(vaug[:, :, :, 2, :], 1.0).then_inc(s2_zero, 1)
            nc.gpsimd.tensor_copy(vaug[:, :, :, 1, :],
                                  kvtok[:, :, 128:256].rearrange("p t (v d) -> p t v d", v=KVH)).then_inc(s2_vaug, 1)
            src = qtok.rearrange("p t (h d) -> p t h d", d=HD)[:, 4:8]
            nc.gpsimd.tensor_tensor(tmpq[:, 4:8], src, src, ALU.mult).then_inc(s2_sq1, 1)
            pool.wait_ge(s2_rec1, 1)
            pool.wait_ge(s2_gain, 32)
            n = norm_rope(pool, nc.gpsimd, s2_p, 0, src, tmpq[:, 4:8], rsh[:, 32:64], qgr, None, 4, QH, 0)
            pool.wait_ge(s2_rope, 16)
            rotate(pool, nc.gpsimd, s2_p, n, src, tmpq[:, 4:8], qn[:, 4:8], 4, 4, QH).then_inc(s2_q1, 1)
            pool.wait_ge(s2_q1, 1)
            done = 0
            for n in range(SPLIT_DVE, JOBS):
                if n == SPLIT_DVE:
                    pool.wait_ge(s2_q0, 1)
                split_queries(pool, nc.gpsimd, n, s2_hi2, s2_qs2, n - SPLIT_DVE)
                for _ in range(2):
                    if done < len(short_ops):
                        short_step(pool, done)
                        done += 1
            while done < len(short_ops):
                short_step(pool, done)
                done += 1

        @b2.vector
        def _(dve):
            step = [0]

            def link(ins):
                step[0] += 1
                bump(dve, s2_v, ins, step[0])

            ksrc = kvtok[:, :, 0:128].rearrange("p t (v d) -> p t v d", v=KVH)
            qsrc = qtok.rearrange("p t (h d) -> p t h d", d=HD)[:, 0:4]
            tk = tmpq[:, 0:4].rearrange("p t h d -> p (t h d)")[:, 0:TA * 128]
            tk4 = tk.rearrange("p (t v d) -> p t v d", v=KVH, d=HD)
            link(nc.vector.tensor_tensor(tk4, ksrc, ksrc, ALU.mult))
            nc.vector.tensor_reduce(ssh[:, 64:84], tk.rearrange("p (t d) -> p t d", d=HD), AX.X, ALU.add
                                    ).then_inc(s2_ssk, 1)
            dve.wait_ge(s2_ssk, 1)
            link(nc.vector.tensor_tensor(tmpq[:, 0:4], qsrc, qsrc, ALU.mult))
            nc.vector.tensor_reduce(ssh[:, 0:32], tmpq[:, 0:4].rearrange("p t h d -> p (t h) d"), AX.X, ALU.add
                                    ).then_inc(s2_ssq, 1)
            dve.wait_ge(s2_ssq, 1)
            dve.wait_ge(s2_gain, 32)
            dve.wait_ge(s2_rope, 16)
            dve.wait_ge(s2_stdk, 1)
            link(nc.vector.reciprocal(rsh[:, 64:84], ssh[:, 64:84]))
            step[0] = norm_rope(dve, nc.vector, s2_v, step[0], ksrc, tk4, rsh[:, 64:84], kgr, None, TA, KVH, 2)
            nc.vector.tensor_copy(kn[:, 0:2], ksrc[:, 0:2])
            last = rotate(dve, nc.vector, s2_v, step[0], ksrc[:, 2:], tk4[:, 2:], kn[:, 2:], 0, NT, KVH)
            step[0] += 1
            last.then_inc(s2_kn, 1)
            dve.wait_ge(s2_kn, 1)
            for v in range(KVH):
                nc.vector.tensor_copy(k_hh[v][:, :, 0:64], kn[:, :, v])
                last = nc.vector.tensor_copy(k_hh[v][:, :, 64:128], kn[:, :, v])
            link(last)
            for v in range(KVH):
                last = nc.vector.tensor_tensor(k_lo[v][:, :, 0:64], kn[:, :, v], k_hh[v][:, :, 0:64], ALU.subtract)
            last.then_inc(s2_k, 1)
            dve.wait_ge(s2_stdq, 1)
            link(nc.vector.reciprocal(rsh[:, 0:32], ssh[:, 0:32]))
            dve.wait_ge(s2_k, 1)
            step[0] = norm_rope(dve, nc.vector, s2_v, step[0], qsrc, tmpq[:, 0:4], rsh[:, 0:32], qgr, None, 4, QH, 0)
            last = rotate(dve, nc.vector, s2_v, step[0], qsrc, tmpq[:, 0:4], qn[:, 0:4], 0, 4, QH)
            step[0] += 1
            last.then_inc(s2_q0, 1)
            dve.wait_ge(s2_q0, 1)
            for n in range(2):
                if n == 1:
                    dve.wait_ge(s2_kt, 12)
                split_queries(dve, nc.vector, n, s2_hi, s2_qs, n)
            dve.wait_ge(s2_sq1, 1)
            nc.vector.tensor_reduce(ssh[:, 32:64], tmpq[:, 4:8].rearrange("p t h d -> p (t h) d"), AX.X, ALU.add
                                    ).then_inc(s2_ssq, 1)
            dve.wait_ge(s2_tapt, 1)
            nc.vector.tensor_copy(dwT, psum[:, 0, 0:2 * CW].rearrange("p (m j) -> p m j", m=2))
            nc.vector.tensor_copy(gwT, psum[:, 0, 64:64 + 6 * SW].rearrange("p (m j) -> p m j", m=6)).then_inc(s2_tapv, 1)
            dve.wait_ge(s2_std1, 1)
            nc.vector.reciprocal(rsh[:, 32:64], ssh[:, 32:64]).then_inc(s2_rec1, 1)
            taps_done = [0]

            def conformer_step():
                n = taps_done[0]
                if n >= len(conf_ops):
                    return
                m, j = conf_ops[n]
                if n == 0:
                    dve.wait_ge(s2_col, 64)
                    dve.wait_ge(s2_tapv, 1)
                    dve.wait_ge(s2_vaug, 1)
                    dve.wait_ge(s2_q1, 1)
                if n >= 2:
                    dve.wait_ge(s2_conv, n - 1)
                if j == 0:
                    ins = nc.vector.tensor_scalar(cacc[:, m, :], cvg[:, m, 0:L], dwT[:, m, 0:1], ccol[:, 0, m:m + 1],
                                                  ALU.mult, ALU.add)
                else:
                    ins = nc.vector.scalar_tensor_tensor(cacc[:, m, :], cvg[:, m, j:j + L], dwT[:, m, j:j + 1],
                                                         cacc[:, m, :], ALU.mult, ALU.add)
                ins.then_inc(s2_conv, 1)
                taps_done[0] += 1

            def maxima(n, items):
                for it in items:
                    t, ch = A_ITEMS[it]
                    k = n * 12 + it
                    dve.wait_ge(s2_a, k + 1)
                    nc.vector.tensor_reduce(pmax[:, n % 4, t, ch:ch + 1], psum[:, k % 3, 0:KCH[ch][1]],
                                            AX.X, ALU.max).then_inc(s2_am, 1)
                if items[-1] == 11:
                    dve.wait_ge(s2_am, 12 * (n + 1))
                    nc.vector.tensor_reduce(nmax[:, n % 4, :], pmax[:, n % 4], AX.X, ALU.max, negate=True
                                            ).then_inc(s2_nm, 1)

            def row_out(n):
                dve.wait_ge(s2_row, n + 1)
                if n >= 3:
                    dve.wait_ge(s2_st, KTL * (n - 2))
                nc.vector.tensor_copy(qTm[64:65, n % 3, :], psum[64:65, 7, :]).then_inc(s2_rowv, 1)

            def finish(n):
                hh, h = divmod(n, QH)
                dve.wait_ge(s2_pv, KTL * (n + 1))
                o, z = (0, 64) if h % 2 == 0 else (64, 0)
                b = psum[:, 5 + n % 2, :]
                inv = at(111.5, 512)
                if n >= 1:
                    dve.wait_ge(s2_o, n)
                nc.vector.reciprocal(inv[o:o + 64], b[z:z + 64]).then_inc(s2_rec, 1)
                dve.wait_ge(s2_rec, n + 1)
                nc.vector.tensor_tensor(attnT[o:o + 64, h // 2, hh * 512:(hh + 1) * 512], b[o:o + 64], inv[o:o + 64],
                                        ALU.mult).then_inc(s2_o, 1)

            maxima(0, list(range(12)))
            row_out(0)
            split_queries(dve, nc.vector, 2, s2_hi, s2_qs, 2)
            maxima(1, list(range(12)))
            split_queries(dve, nc.vector, 3, s2_hi, s2_qs, 3)
            for n in range(JOBS):
                if n >= 1:
                    finish(n - 1)
                for k in range(4):
                    if n + 2 < JOBS:
                        maxima(n + 2, list(range(3 * k, 3 * k + 3)))
                    if k == 0 and n + 1 < JOBS:
                        row_out(n + 1)
                    conformer_step()
            finish(JOBS - 1)
            while taps_done[0] < len(conf_ops):
                conformer_step()
            for t in range(NT):
                dve.wait_ge(s2_ct, t + 1)
                v = psum[:, t % 4, 0:256]
                nc.vector.bn_stats(stats[:, t, 0:6], v).then_inc(s2_bn, 1)
                dve.wait_ge(s2_bn, 3 * t + 1)
                nc.vector.bn_aggr(mv[:, t, :], stats[:, t, 0:6]).then_inc(s2_bn, 1)
                dve.wait_ge(s2_bn, 3 * t + 2)
                nc.vector.tensor_scalar(xtok[:, t, :], v, mv[:, t, 0:1], None, ALU.subtract).then_inc(s2_bn, 1)
            dve.wait_ge(s2_lstd, 1)
            link(nc.vector.reciprocal(lrs, lrs))
            for t in range(NT):
                nc.vector.tensor_scalar(xtok[:, t, :], xtok[:, t, :], lrs[:, t:t + 1], None, ALU.mult).then_inc(s2_ln, 1)
            for n in range(4):
                m, hh = divmod(n, 2)
                dve.wait_ge(s2_pwm, n + 1)
                nc.vector.tensor_scalar(convT[:, m, hh * 512:(hh + 1) * 512], psum[:, 4 + n, :], ccol[:, 3, m:m + 1], None,
                                        ALU.add).then_inc(s2_out, 1)

        @b2.scalar
        def _(act):
            act.wait_ge(s2_zo, 1)
            act.wait_ge(s2_ssk, 1)
            nc.scalar.activation(ssh[:, 64:84], ssh[:, 64:84], ACT.Sqrt, bias=eps64[:, 0:1], scale=1.0 / HD).then_inc(s2_stdk, 1)
            act.wait_ge(s2_ssq, 1)
            nc.scalar.activation(ssh[:, 0:32], ssh[:, 0:32], ACT.Sqrt, bias=eps64[:, 1:2], scale=1.0).then_inc(s2_stdq, 1)
            nc.scalar.activation(qTm, zero_one[:, 0:1].unsqueeze(1).broadcast_to([P, 3, 512]), ACT.Copy).then_inc(s2_qz, 1)
            for g in range(12):
                act.wait_ge(s2_kt, g + 1)
                v, ch = divmod(g % 6, 3)
                o, w = KCH[ch]
                nc.scalar.activation((kTh, kTl)[g // 6][:, v, o:o + w], psum[:, 1 + g % 6, 0:w], ACT.Copy
                                     ).then_inc(s2_ktv, 1)
            act.wait_ge(s2_ssq, 2)
            nc.scalar.activation(ssh[:, 32:64], ssh[:, 32:64], ACT.Sqrt, bias=eps64[:, 1:2], scale=1.0).then_inc(s2_std1, 1)

            def queries(n):
                act.wait_ge(s2_t, n + 1)
                if n >= 3:
                    act.wait_ge(s2_st, KTL * (n - 2))
                nc.scalar.activation(qT2[:, n % 3, :], psum[:, 7, :], ACT.Copy)
                nc.scalar.activation(qTm[0:64, n % 3, :], psum[0:64, 7, :], ACT.Copy).then_inc(s2_qt, 1)

            def weights(g):
                act.wait_ge(s2_st, g + 1)
                if g >= 4:
                    act.wait_ge(s2_pv, g - 3)
                nc.scalar.activation(pT[:, g % 4, :], psum[:, 3 + g % 2, :], ACT.Exp).then_inc(s2_exp, 1)

            def copy_back(i):
                act.wait_ge(s2_sconv, 10 * (i + 1))
                for m in (2 * i, 2 * i + 1):
                    nc.scalar.activation(qkvT[:, m, 0:1284], sacc[:, m % 2, :], ACT.Copy).then_inc(s2_back, 1)

            act.wait_ge(s2_qz, 1)
            queries(0)
            queries(1)
            for n in range(JOBS):
                if n in (5, 10):
                    copy_back(n // 5 - 1)
                for j in range(KTL):
                    weights(n * KTL + j)
                    if j == 1 and n + 2 < JOBS:
                        queries(n + 2)
            copy_back(2)
            act.wait_ge(s2_back, 6)
            for m in range(6):
                nc.scalar.activation(qkvT[:, m, 0:1284], qkvT[:, m, 0:1284], ACT.Silu).then_inc(s2_silu, 1)
            act.wait_ge(s2_bn, 3 * NT)
            nc.scalar.activation(lrs, mv[:, :, 1], ACT.Sqrt, bias=eps64[:, 0:1]).then_inc(s2_lstd, 1)
            for n in range(4):
                m, hh = divmod(n, 2)
                act.wait_ge(s2_hT, n + 1)
                nc.scalar.activation(hcT[:, m, hh * 512:(hh + 1) * 512], psum[:, 4 + n, :], ACT.Silu,
                                     bias=ccol[:, 2, m:m + 1], scale=ccol[:, 1, m:m + 1]).then_inc(s2_hc, 1)

        @b2.tensor
        def _(pe):
            pe.wait_ge(s2_tap, 32)
            for m in range(2):
                nc.tensor.transpose(psum[:, 0, m * CW:(m + 1) * CW], wtap_r[0:CW, m * P:(m + 1) * P], ident[0:CW, 0:CW])
            for m in range(6):
                last = nc.tensor.transpose(psum[:, 0, 64 + m * SW:64 + (m + 1) * SW],
                                           wtap_r[0:SW, 256 + m * P:256 + (m + 1) * P], ident[0:SW, 0:SW])
            last.then_inc(s2_tapt, 1)
            pe.wait_ge(s2_k, 1)
            pe.wait_ge(s2_zero, 1)
            for g in range(12):
                v, ch = divmod(g % 6, 3)
                if g >= 6:
                    pe.wait_ge(s2_ktv, g - 5)
                for i in range(KCH[ch][1] // P):
                    last = nc.tensor.matmul(psum[:, 1 + g % 6, i * P:(i + 1) * P],
                                            (k_hh, k_lo)[g // 6][v][:, 4 * ch + i, :], idr, start=True, stop=True)
                last.then_inc(s2_kt, 1)

            def turn(n):
                hh, h = divmod(n, QH)
                if n < SPLIT_DVE:
                    pe.wait_ge(s2_qs, n + 1)
                else:
                    pe.wait_ge(s2_qs2, n - SPLIT_DVE + 1)
                if n >= 2:
                    pe.wait_ge(s2_rowv, n - 1)
                elif n:
                    pe.wait_ge(s2_rowv, 1)
                for t in range(4):
                    last = nc.tensor.matmul(psum[:, 7, t * P:(t + 1) * P], q_hl[n % 2][:, t], idr,
                                            start=True, stop=True)
                last.then_inc(s2_t, 1)

            def scores_for_max(n, items):
                h = n % QH
                for it in items:
                    t, ch = A_ITEMS[it]
                    k = n * 12 + it
                    if it == 0:
                        pe.wait_ge(s2_qt, n + 1)
                    if k >= 3:
                        pe.wait_ge(s2_am, k - 2)
                    o, w = KCH[ch]
                    nc.tensor.matmul(psum[:, k % 3, 0:w], qT2[:, n % 3, t * P:(t + 1) * P],
                                     kTh[:, h // 4, o:o + w], start=True, stop=True).then_inc(s2_a, 1)

            def max_row(n):
                pe.wait_ge(s2_nm, n + 1)
                if n + 2 <= JOBS:
                    pe.wait_ge(s2_qt, min(n + 2, JOBS) if n else 1)
                for t in range(4):
                    last = nc.tensor.matmul(psum[64:65, 7, t * P:(t + 1) * P], nmax[:, n % 4, t:t + 1], ident,
                                            start=True, stop=True)
                last.then_inc(s2_row, 1)

            def values(g):
                n, j = divmod(g, KTL)
                h = n % QH
                pe.wait_ge(s2_exp, g + 1)
                if j == 0 and n >= 2:
                    pe.wait_ge(s2_o, n - 1)
                o = 1 if h % 2 == 0 else 0
                nc.tensor.matmul(psum[:, 5 + n % 2, :], vaug[:, j, h // 4, o:o + 2, :].rearrange("p a d -> p (a d)"),
                                 pT[:, g % 4, :], start=j == 0, stop=j == KTL - 1).then_inc(s2_pv, 1)

            pe.wait_ge(s2_ktv, 6)
            pe.wait_ge(s2_tapv, 1)
            pe.wait_ge(s2_vaug, 1)
            turn(0)
            scores_for_max(0, list(range(12)))
            max_row(0)
            turn(1)
            scores_for_max(1, list(range(12)))
            for n in range(JOBS):
                if n + 2 < JOBS:
                    turn(n + 2)
                for j in range(KTL):
                    g = n * KTL + j
                    if j == 0:
                        pe.wait_ge(s2_rowv, n + 1)
                        pe.wait_ge(s2_qt, n + 1)
                    if g >= 2:
                        pe.wait_ge(s2_exp, g - 1)
                    keys = slice(j * P, (j + 1) * P)
                    nc.tensor.matmul(psum[:, 3 + g % 2, :], kTh[:, n % QH // 4, keys], qT2[:, n % 3, :],
                                     start=True, stop=False)
                    nc.tensor.matmul(psum[:, 3 + g % 2, :], kTl[:, n % QH // 4, keys], qTm[:, n % 3, :],
                                     start=False, stop=True).then_inc(s2_st, 1)
                    if j == 4 and n + 1 < JOBS:
                        max_row(n + 1)
                    if j >= 4 and n + 2 < JOBS:
                        scores_for_max(n + 2, [2 * (j - 4), 2 * (j - 4) + 1])
                    if g >= 1:
                        values(g - 1)
            values(JOBS * KTL - 1)
            pe.wait_ge(s2_conv, len(conf_ops))
            pe.wait_ge(s2_am, 12 * JOBS)
            for t in range(NT):
                if t >= 4:
                    pe.wait_ge(s2_bn, 3 * (t - 3))
                for m in range(2):
                    last = nc.tensor.transpose(psum[:, t % 4, m * P:(m + 1) * P], cacc[:, m, t * P:(t + 1) * P], ident)
                last.then_inc(s2_ct, 1)
            pe.wait_ge(s2_ln, NT)
            pe.wait_ge(s2_o, JOBS)
            for n in range(4):
                m, hh = divmod(n, 2)
                for t in range(4):
                    last = nc.tensor.transpose(psum[:, 4 + n, t * P:(t + 1) * P],
                                               xtok[:, hh * 4 + t, m * P:(m + 1) * P], ident)
                last.then_inc(s2_hT, 1)
            pe.wait_ge(s2_hc, 4)
            pe.wait_ge(s2_pw, 16)
            for n in range(4):
                m, hh = divmod(n, 2)
                for k in range(2):
                    last = nc.tensor.matmul(psum[:, 4 + n, :], wpw[:, k, m * P:(m + 1) * P],
                                            hcT[:, k, hh * 512:(hh + 1) * 512], start=k == 0, stop=k == 1)
                last.then_inc(s2_pwm, 1)

        middle.close()

        tok = at(41, TA, 3, NH, HD)
        u_all = at(71, TA, 2, NH, HD)
        wT_all = at(91, TA, NH, P)
        qgT_all = at(111, NT, NH, P)
        pT_all = at(0, NT, 2, NH * HD)
        kqT, kP = at(149, 2, 4, P), at(153, 2, NH, P)
        A_ = at(157, 2, 2, NH, P)
        M_ = at(165, 2, 2, NH, P)
        X_, XT_, WT_ = at(173, 2, NH, P), at(177, 2, NH, P), at(181, 2, NH, P)
        E1, gU = at(185, 2, NH, P), at(189, 2, NH, P)
        kvb = at(127, 2, NH, P)
        qg = at(131, NH, 2, HD)
        m_lev, m_pre = at(133, 12, P), at(139, 2, P)
        m_strict, m_incl = at(16, 2, P), at(193, 2, P)
        sqt = at(157, TA, 512)
        onesf = at(140, P)
        AB = TA * 16
        o = 194.75
        ab = at(o, TA, 16)
        gx, gy, gz = at(o + .625, TA, 2, NH), at(o + .9375, TA, 2, NH), at(o + 1.25, TA, 2, NH)
        beta, bexp = at(o + 1.5625, TA, 2, NH), at(o + 1.875, TA, 2, NH)
        gam, egam, ekd = at(o + 2.1875, TA, 2, NH), at(o + 2.5, TA, 2, NH), at(o + 2.8125, TA, 2, NH)
        glb = at(o + 3.125, 2, TA, NH)
        ssn = at(o + 3.4375, TA * 8)
        arow, dtrow = at(o + 3.75, 8), at(o + 3.78125, 8)
        gnr = at(o + 3.8125, HD)
        oss = at(o + 4.0625, NT * NH)
        e2 = at(o + 4.1875, 2)
        S_ = at(127, 2, NH, HD)
        Sg = at(129, NH, HD)
        vn, kd = at(130, 2, NH, HD), at(185, 2, NH, HD)
        o1s = at(187, 2, NH, HD)
        o_f = at(157, 2, NT, NH * HD)
        otok = at(41, NT, NH, HD)
        osq = at(49, NT, NH, HD)
        gdnT = at(57, 2, L)

        third = ExitStack()
        b3 = third.enter_context(nc.Block())
        def sems(names):
            return (sem("s3_" + n) for n in names.split())

        s3_cst, s3_row, s3_one = sems("cst row one")
        s3_tr, s3_tra, s3_trd, s3_ab, s3_abv = sems("tr tra trd ab abv")
        s3_v, s3_a = sems("v a")
        s3_x, s3_sig, s3_abs, s3_g, s3_ssn, s3_stdn, s3_norm = sems("x sig abs g ssn stdn norm")
        s3_pre, s3_prev, s3_gl, s3_eg = sems("pre prev gl eg")
        s3_kq, s3_kqv, s3_G, s3_gU, s3_gb, s3_B, s3_D, s3_E = sems("kq kqv G gU gb B D E")
        s3_AG, s3_A, s3_Q, s3_PT, s3_qg, s3_qgt, s3_qgv = sems("AG A Q PT qg qgt qgv")
        s3_M = [sem("s3_M0"), sem("s3_M1")]
        s3_WT, s3_WTv, s3_X, s3_R, s3_XT = sems("WT WTv X R XT")
        s3_kvb, s3_w, s3_wv, s3_u, s3_uv = sems("kvb w wv u uv")

        def n_wt(t, lev, d):
            return 2 * (6 * t + lev) + d + 1

        def n_r(t, lev, d):
            return 2 * (5 * t + lev - 1) + d + 1

        def n_x(t, lev, d):
            return 2 * (5 * t + lev) + d + 1

        def lat(t):
            return t >= NCT

        def heads(v):
            return v.unsqueeze(2).broadcast_to([v.shape[0], NH, HD])

        def wide(v):
            return v.unsqueeze(2).broadcast_to([P, NH, P])

        def over_heads(m):
            return m.unsqueeze(1).broadcast_to([P, NH, P])

        def schedule(level, stage, outputs):
            for s in range(1, 6):
                stage(0, s)
            for t in range(TA):
                for lev in range(6):
                    level(t, lev)
                    if lev < 5 and t + 1 < TA:
                        stage(t + 1, lev + 1)
                outputs(t)

        @b3.sync
        def _(sp):
            sp.dma_start(m_lev, cst[:, M_LEV * P:(M_LEV + 12) * P].rearrange("p (a n) -> p a n", a=12)).then_inc(s3_cst, 16)
            sp.dma_start(m_pre, cst[:, M_PRE * P:(M_PRE + 2) * P].rearrange("p (a n) -> p a n", a=2)).then_inc(s3_cst, 16)
            sp.dma_start(m_strict, cst[:, M_STRICT * P:(M_STRICT + 2) * P].rearrange("p (a n) -> p a n", a=2)).then_inc(s3_cst, 16)
            sp.dma_start(m_incl, cst[:, M_INCL * P:(M_INCL + 2) * P].rearrange("p (a n) -> p a n", a=2)).then_inc(s3_cst, 16)
            sp.wait_ge(s3_abv, 1)
            sp.dma_start(arow, drow(gdn_a_log)).then_inc(s3_row, 16)
            sp.dma_start(dtrow, drow(gdn_dt_bias)).then_inc(s3_row, 16)
            sp.dma_start(gnr, drow(gdn_norm_g)).then_inc(s3_row, 16)

        @b3.gpsimd
        def _(pool):
            nc.gpsimd.memset(onesf, 1.0).then_inc(s3_one, 1)
            pool.wait_ge(s3_tr, 2 * TA)
            nc.gpsimd.memset(kP, 0.0).then_inc(s3_one, 1)
            pool.wait_ge(s3_abv, 1)
            nc.gpsimd.memset(e2[:, 0:1], EPS)
            nc.gpsimd.memset(e2[:, 1:2], 64 * EPS).then_inc(s3_one, 1)
            pool.wait_ge(s3_cst, 64)
            pool.wait_ge(s3_g, 1)
            pool.wait_ge(s3_eg, 4)
            pool.wait_ge(s3_norm, 2)

            def stage(t, s):
                if s == 1:
                    for d in range(2):
                        if t:
                            pool.wait_ge(s3_gb, 2 * (t - 1) + d + 1)
                        nc.gpsimd.tensor_tensor(gU[:, d], over_heads(m_pre[:, d]), wide(gx[:, t, d]), ALU.mult
                                                ).then_inc(s3_gU, 1)
                if s == 2:
                    for d in range(2):
                        pool.wait_ge(s3_B, 2 * t + d + 1)
                        nc.gpsimd.tensor_tensor(A_[:, t % 2, d], over_heads(m_strict[:, d]), E1[:, d], ALU.subtract)
                        nc.gpsimd.tensor_tensor(E1[:, d], E1[:, d], over_heads(m_incl[:, d]), ALU.add).then_inc(s3_D, 1)
                if s == 3:
                    for d in range(2):
                        pool.wait_ge(s3_AG, 2 * t + d + 1)
                        nc.gpsimd.tensor_tensor(A_[:, t % 2, d], A_[:, t % 2, d], wide(beta[:, t, d]), ALU.mult
                                                ).then_inc(s3_A, 1)
                if s == 4 and lat(t):
                    if t > NCT:
                        pool.wait_ge(s3_qgt, t - NCT)
                    for d in range(2):
                        last = nc.gpsimd.tensor_tensor(qg[:, :, d, :], tok[:, t, 0], heads(egam[:, t, d]), ALU.mult)
                    last.then_inc(s3_qg, 1)

            def mask(t, lev):
                for d in range(2):
                    n = 6 * t + lev
                    if lev == 0:
                        pool.wait_ge(s3_A, 2 * t + d + 1)
                    if n >= 2:
                        t2, l2 = divmod(n - 2, 6)
                        pool.wait_ge(s3_WT, n_wt(t2, l2, d))
                        if l2 == 0:
                            pool.wait_ge(s3_X, n_x(t2, 0, d))
                    nc.gpsimd.tensor_tensor(M_[:, d, n % 2], A_[:, t % 2, d], over_heads(m_lev[:, d * 6 + lev]), ALU.mult
                                            ).then_inc(s3_M[d], 1)

            def products(t):
                for d in range(2):
                    if t:
                        pool.wait_ge(s3_u, 2 * (t - 1) + d + 1)
                    nc.gpsimd.tensor_tensor(kvb[:, d, :, 0:64], tok[:, t, 1], heads(bexp[:, t, d]), ALU.mult)
                    nc.gpsimd.tensor_tensor(kvb[:, d, :, 64:128], tok[:, t, 2], heads(beta[:, t, d]), ALU.mult
                                            ).then_inc(s3_kvb, 1)

            def level(t, lev):
                if lev == 0 and t == 0:
                    mask(t, 0)
                if lev < 5:
                    mask(t, lev + 1)
                if lev == 1:
                    products(t)

            def outputs(t):
                if t + 1 < TA:
                    mask(t + 1, 0)

            schedule(level, stage, outputs)

        @b3.scalar
        def _(act):
            for t in range(TA):
                act.wait_ge(s3_tr, 2 * t + 1)
                nc.scalar.activation(tok[:, t, 0:2].rearrange("p a h d -> p (a h d)"), psum[:, 2 * t % 4, :], ACT.Copy
                                     ).then_inc(s3_tra, 1)
            link = [0]

            def chain(ins):
                link[0] += 1
                bump(act, s3_a, ins, link[0])

            act.wait_ge(s3_x, 1)
            act.wait_ge(s3_one, 3)
            nc.scalar.activation(beta, ab[:, :, 8:16].rearrange("p t (d h) -> p t d h", d=2), ACT.Sigmoid).then_inc(s3_sig, 1)
            chain(nc.scalar.activation(gy, gx, ACT.Abs))
            chain(nc.scalar.activation(gy, gy, ACT.Exp, scale=-1.0))
            nc.scalar.activation(arow, arow, ACT.Exp)
            nc.scalar.activation(gy, gy, ACT.Ln, bias=1.0).then_inc(s3_abs, 1)
            act.wait_ge(s3_ssn, 1)
            v = ssn.rearrange("p (t a h) -> p t a h", a=2, h=NH)
            nc.scalar.activation(v[:, :, 0], v[:, :, 0], ACT.Sqrt, bias=e2[:, 1:2], scale=float(HD))
            nc.scalar.activation(v[:, :, 1], v[:, :, 1], ACT.Sqrt, bias=e2[:, 0:1], scale=1.0).then_inc(s3_stdn, 1)
            act.wait_ge(s3_pre, 2)
            for d in range(2):
                r = slice(64 * d, 64 * d + 64)
                for c_ in range(2):
                    nc.scalar.activation(glb[r, c_], psum[r, 6 + c_, 0:TA * NH].rearrange("p (t h) -> p t h", h=NH),
                                         ACT.Exp).then_inc(s3_gl, 1)
            act.wait_ge(s3_prev, 3)
            nc.scalar.activation(egam, gam, ACT.Exp).then_inc(s3_eg, 1)
            nc.scalar.activation(ekd, ekd, ACT.Exp).then_inc(s3_eg, 1)

            def stage(t, s):
                b6 = psum[:, 6, :].rearrange("p (a n) -> p a n", a=4)
                if s == 1:
                    act.wait_ge(s3_kq, t + 1)
                    if t >= 2:
                        act.wait_ge(s3_G, t - 1)
                        if lat(t - 2):
                            act.wait_ge(s3_Q, t - 1 - NCT)
                    elif t == 0:
                        act.wait_ge(s3_one, 3)
                    nc.scalar.activation(kqT[:, t % 2], b6, ACT.Copy)
                    nc.scalar.activation(kP[0:64, t % 2, 0:4:2], b6[0:64, 0:2], ACT.Copy)
                    nc.scalar.activation(kP[64:128, t % 2, 1:4:2], b6[64:128, 0:2], ACT.Copy).then_inc(s3_kqv, 1)
                if s == 3:
                    for d in range(2):
                        act.wait_ge(s3_D, 2 * t + d + 1)
                        nc.scalar.activation(A_[:, t % 2, d], A_[:, t % 2, d], ACT.Exp).then_inc(s3_E, 1)
                        nc.scalar.activation(E1[:, d], E1[:, d], ACT.Exp).then_inc(s3_E, 1)
                if s == 5 and lat(t):
                    act.wait_ge(s3_qgt, t + 1 - NCT)
                    nc.scalar.activation(qgT_all[:, t - NCT], b6, ACT.Copy).then_inc(s3_qgv, 1)

            def level(t, lev):
                if lev == 0:
                    return
                for d in range(2):
                    act.wait_ge(s3_WT, n_wt(t, lev, d))
                    if n_r(t, lev, d) > 2:
                        act.wait_ge(s3_R, n_r(t, lev, d) - 2)
                    nc.scalar.activation(WT_[:, d], psum[:, 3 * d, :].rearrange("p (h n) -> p h n", h=NH), ACT.Copy
                                         ).then_inc(s3_WTv, 1)

            def outputs(t):
                for d in range(2):
                    r = slice(64 * d, 64 * d + 64)
                    act.wait_ge(s3_w, 2 * t + d + 1)
                    nc.scalar.activation(wT_all[r, t], psum[r, 3 * d + 1, :].rearrange("p (h n) -> p h n", h=NH), ACT.Copy
                                         ).then_inc(s3_wv, 1)

            schedule(level, stage, outputs)

        @b3.vector
        def _(dve):
            for t in range(TA):
                dve.wait_ge(s3_tr, 2 * t + 2)
                nc.vector.tensor_copy(tok[:, t, 2].rearrange("p h d -> p (h d)"), psum[:, (2 * t + 1) % 4, 0:256]
                                      ).then_inc(s3_trd, 1)
            dve.wait_ge(s3_ab, 1)
            nc.vector.tensor_copy(ab, psum[:, 5, 0:AB].rearrange("p (t n) -> p t n", n=16)).then_inc(s3_abv, 1)
            link = [0]

            def chain(ins):
                link[0] += 1
                bump(dve, s3_v, ins, link[0])

            dve.wait_ge(s3_abv, 1)
            dve.wait_ge(s3_row, 48)
            ax = ab[:, :, 0:8].rearrange("p t (d h) -> p t d h", d=2)
            db = dtrow.rearrange("p (d h) -> p d h", d=2).unsqueeze(1).broadcast_to([P, TA, 2, NH])
            nb = arow.rearrange("p (d h) -> p d h", d=2).unsqueeze(1).broadcast_to([P, TA, 2, NH])
            nc.vector.tensor_tensor(gx, ax, db, ALU.add).then_inc(s3_x, 1)
            dve.wait_ge(s3_tra, TA)
            dve.wait_ge(s3_tr, 2 * TA)
            qk = tok[:, :, 0:2].rearrange("p t a h d -> p t (a h d)")
            chain(nc.vector.tensor_tensor(sqt, qk, qk, ALU.mult))
            nc.vector.tensor_reduce(ssn, sqt.rearrange("p t (a d) -> p (t a) d", d=HD), AX.X, ALU.add).then_inc(s3_ssn, 1)
            dve.wait_ge(s3_abs, 1)
            chain(nc.vector.tensor_scalar(gz, gx, 0.0, None, ALU.max))
            chain(nc.vector.tensor_tensor(gz, gz, gy, ALU.add))
            chain(nc.vector.tensor_tensor(gz, gz, nb, ALU.mult))
            nc.vector.tensor_scalar(gx, gz, -1.0, None, ALU.mult).then_inc(s3_g, 1)
            dve.wait_ge(s3_stdn, 1)
            chain(nc.vector.reciprocal(ssn, ssn))
            for t in range(TA):
                v = tok[:, t, 0:2].rearrange("p a h d -> p (a h) d")
                last = nc.vector.tensor_tensor(v, v, ssn[:, 8 * t:8 * t + 8].unsqueeze(2).broadcast_to([P, 8, HD]), ALU.mult)
            last.then_inc(s3_norm, 2)
            dve.wait_ge(s3_pre, 1)
            for d in range(2):
                same = psum[:, 4, d * 80:d * 80 + 80].rearrange("p (t e h) -> p t e h", e=2, h=NH)
                nc.vector.tensor_copy(gam[:, :, d], same[:, :, d])
                last = nc.vector.tensor_tensor(ekd[:, :, 1 - d], same[:, :, 1 - d], gx[:, :, 1 - d], ALU.subtract)
            last.then_inc(s3_prev, 3)
            dve.wait_ge(s3_eg, 2)
            dve.wait_ge(s3_sig, 1)
            nc.vector.tensor_tensor(bexp, beta, egam, ALU.mult).then_inc(s3_eg, 2)
            dve.wait_ge(s3_cst, 64)

            def bank(b):
                return psum[:, b, :].rearrange("p (h n) -> p h n", h=NH)

            def stage(t, s):
                if s == 2:
                    for d in range(2):
                        dve.wait_ge(s3_gb, 2 * t + d + 1)
                        if t:
                            dve.wait_ge(s3_E, 4 * (t - 1) + 2 * d + 2)
                            if lat(t - 1):
                                dve.wait_ge(s3_PT, 2 * (t - 1 - NCT) + d + 1)
                        nc.vector.tensor_tensor(E1[:, d], bank(6), wide(gam[:, t, d]), ALU.subtract).then_inc(s3_B, 1)
                if s == 3:
                    dve.wait_ge(s3_G, t + 1)
                    for d in range(2):
                        dve.wait_ge(s3_E, 4 * t + 2 * d + 1)
                        nc.vector.tensor_tensor(A_[:, t % 2, d], A_[:, t % 2, d], bank(7), ALU.mult).then_inc(s3_AG, 1)
                if s == 4 and lat(t):
                    dve.wait_ge(s3_Q, t + 1 - NCT)
                    for d in range(2):
                        dve.wait_ge(s3_E, 4 * t + 2 * d + 2)
                        for c_ in range(2):
                            r = slice(64 * c_, 64 * c_ + 64)
                            last = nc.vector.tensor_tensor(
                                pT_all[r, t - NCT, d].rearrange("p (h n) -> p h n", h=NH),
                                bank(7)[r, :, r], E1[r, d, :, r], ALU.mult)
                        last.then_inc(s3_PT, 1)

            def level(t, lev):
                for d in range(2):
                    if lev == 0:
                        dve.wait_ge(s3_M[d], 6 * t + 1)
                        if t:
                            dve.wait_ge(s3_u, 2 * (t - 1) + d + 1)
                        nc.vector.tensor_tensor(X_[:, d], over_heads(ident), M_[:, d, 6 * t % 2], ALU.subtract
                                                ).then_inc(s3_X, 1)
                        dve.wait_ge(s3_WT, n_wt(t, 0, d))
                        nc.vector.tensor_tensor(XT_[:, d], over_heads(ident), bank(3 * d), ALU.subtract).then_inc(s3_XT, 1)
                        continue
                    dve.wait_ge(s3_R, n_r(t, lev, d))
                    if lev < 5:
                        nc.vector.tensor_tensor(X_[:, d], X_[:, d], bank(3 * d + 1), ALU.subtract).then_inc(s3_X, 1)
                    nc.vector.tensor_tensor(XT_[:, d], XT_[:, d], bank(3 * d + 2), ALU.subtract).then_inc(s3_XT, 1)

            def outputs(t):
                for d in range(2):
                    dve.wait_ge(s3_u, 2 * t + d + 1)
                    nc.vector.tensor_copy(u_all[:, t, d], bank(3 * d + 2)[:, :, 64:128]).then_inc(s3_uv, 1)

            schedule(level, stage, outputs)

        @b3.tensor
        def _(pe):
            for t in range(TA):
                o = t * P + (4 if lat(t) else 0)
                if t >= 2:
                    pe.wait_ge(s3_tra, t - 1)
                    pe.wait_ge(s3_trd, t - 1)
                for m in range(4):
                    last = nc.tensor.transpose(psum[:, 2 * t % 4, m * P:(m + 1) * P], qkvT[:, m, o:o + P], ident)
                last.then_inc(s3_tr, 1)
                for m in range(2):
                    last = nc.tensor.transpose(psum[:, (2 * t + 1) % 4, m * P:(m + 1) * P], qkvT[:, 4 + m, o:o + P], ident)
                last.then_inc(s3_tr, 1)
            for t in range(TA):
                last = nc.tensor.transpose(psum[:, 5, t * 16:(t + 1) * 16], abT[0:16, t * P:(t + 1) * P], ident[0:16, 0:16])
            last.then_inc(s3_ab, 1)
            pe.wait_ge(s3_g, 1)
            pe.wait_ge(s3_cst, 64)
            pe.wait_ge(s3_one, 1)
            gr = gx.rearrange("p t d h -> p (t d h)")
            for d in range(2):
                last = nc.tensor.matmul(psum[:, 4, d * 80:d * 80 + 80], m_pre[:, d], gr, start=True, stop=True)
            last.then_inc(s3_pre, 1)
            for c_ in range(2):
                r = slice(64 * c_, 64 * c_ + 64)
                for d in range(2):
                    last = nc.tensor.matmul(psum[64 * d:64 * d + 64, 6 + c_, 0:TA * NH].rearrange("p (t h) -> p t h", h=NH),
                                            onesf[r, 0:64], gx[r, :, d], start=True, stop=True)
            last.then_inc(s3_pre, 1)
            pe.wait_ge(s3_norm, 1)
            pe.wait_ge(s3_gl, 4)

            def stage(t, s):
                if s == 1:
                    if t:
                        if lat(t - 1):
                            pe.wait_ge(s3_qgv, t - NCT)
                        else:
                            pe.wait_ge(s3_B, 2 * t)
                    for a in range(2):
                        for m in range(2):
                            src = tok[:, t, 1 - a].rearrange("p h d -> p (h d)")[:, m * P:(m + 1) * P]
                            i = 2 * a + m
                            last = nc.tensor.transpose(psum[:, 6, i * P:(i + 1) * P], src, ident)
                    last.then_inc(s3_kq, 1)
                if s == 2:
                    pe.wait_ge(s3_kqv, t + 1)
                    if t:
                        if lat(t - 1):
                            pe.wait_ge(s3_PT, 2 * (t - NCT))
                        else:
                            pe.wait_ge(s3_AG, 2 * t)
                    for h in range(NH):
                        last = nc.tensor.matmul(psum[:, 7, h * P:(h + 1) * P], kP[:, t % 2, h], kqT[:, t % 2, h // 2],
                                                start=True, stop=True)
                    last.then_inc(s3_G, 1)
                    for d in range(2):
                        pe.wait_ge(s3_gU, 2 * t + d + 1)
                        if d:
                            pe.wait_ge(s3_B, 2 * t + 1)
                        nc.tensor.matmul(psum[:, 6, :], onesf, gU[:, d].rearrange("p h n -> p (h n)"),
                                         start=True, stop=True).then_inc(s3_gb, 1)
                if s == 4 and lat(t):
                    pe.wait_ge(s3_AG, 2 * t + 2)
                    for h in range(NH):
                        last = nc.tensor.matmul(psum[:, 7, h * P:(h + 1) * P], kP[:, t % 2, h], kqT[:, t % 2, 2 + h // 2],
                                                start=True, stop=True)
                    last.then_inc(s3_Q, 1)
                if s == 5 and lat(t):
                    pe.wait_ge(s3_qg, t + 1 - NCT)
                    pe.wait_ge(s3_B, 2 * t + 2)
                    for h in range(NH):
                        last = nc.tensor.transpose(psum[:, 6, h * P:(h + 1) * P], qg[:, h].rearrange("p d n -> p (d n)"), ident)
                    last.then_inc(s3_qgt, 1)

            def four(b, lhs, rhs):
                for h in range(NH):
                    last = nc.tensor.matmul(psum[:, b, h * P:(h + 1) * P], lhs(h), rhs(h), start=True, stop=True)
                return last

            def level(t, lev):
                n = 6 * t + lev
                for d in range(2):
                    pe.wait_ge(s3_M[d], n + 1)
                    if lev:
                        pe.wait_ge(s3_XT, n_wt(t, lev - 1, d))
                    elif t:
                        pe.wait_ge(s3_WTv, n_r(t - 1, 5, d))
                    if lev:
                        last = four(3 * d, lambda h: M_[:, d, n % 2, h], lambda h: XT_[:, d, h])
                    else:
                        for h in range(NH):
                            last = nc.tensor.transpose(psum[:, 3 * d, h * P:(h + 1) * P], M_[:, d, n % 2, h], ident)
                    last.then_inc(s3_WT, 1)
                if lev == 0:
                    return
                for d in range(2):
                    pe.wait_ge(s3_WTv, n_r(t, lev, d))
                    pe.wait_ge(s3_X, n_x(t, lev - 1, d))
                    if lev == 1 and t:
                        pe.wait_ge(s3_wv, 2 * (t - 1) + d + 1)
                        pe.wait_ge(s3_uv, 2 * (t - 1) + d + 1)
                    if lev < 5:
                        four(3 * d + 1, lambda h: WT_[:, d, h], lambda h: X_[:, d, h])
                    four(3 * d + 2, lambda h: X_[:, d, h], lambda h: WT_[:, d, h]).then_inc(s3_R, 1)

            def outputs(t):
                for d in range(2):
                    pe.wait_ge(s3_kvb, 2 * t + d + 1)
                    pe.wait_ge(s3_XT, n_wt(t, 5, d))
                    for h in range(NH):
                        last = nc.tensor.matmul(psum[64 * d:64 * d + 64, 3 * d + 1, h * P:(h + 1) * P],
                                                kvb[:, d, h, 0:64], XT_[:, d, h], start=True, stop=True)
                    last.then_inc(s3_w, 1)
                    four(3 * d + 2, lambda h: XT_[:, d, h], lambda h: kvb[:, d, h]).then_inc(s3_u, 1)

            schedule(level, stage, outputs)

        third.close()
        retire_semaphores()

        STEPS = 2 * TA
        wo_kb = (133, 137, 149, 153, 173, 177, 181, 189)
        wo = [at(kb, D) for kb in wo_kb]
        x1 = at(65, NT, D)
        gate1 = at(97, D)
        xr = at(101, NT, D)

        def chunk_of(i, d):
            g = i if d == 0 else (3 - i if i < 4 else 23 - i)
            return g // 2, g % 2

        xn = [at(4 * t if t < 4 else 25 + 4 * t, D) for t in range(NT)]

        fourth = ExitStack()
        b4 = fourth.enter_context(nc.Block())

        def sems4(names):
            return (sem("s4_" + n) for n in names.split())

        s4_wo, s4_x, s4_g1 = sems4("wo x g1")
        s4_zero, s4_kd, s4_wS, s4_vn, s4_up, s4_S, s4_Sg, s4_o1, s4_o1c, s4_o2, s4_o = sems4(
            "zero kd wS vn up S Sg o1 o1c o2 o")
        s4_v, s4_oss, s4_std, s4_y, s4_yt, s4_yv, s4_mm, s4_ev, s4_res = sems4("v oss std y yt yv mm ev res")

        zrow = at(16, 256)
        s4_zrow, s4_fill = sems4("zrow fill")
        s4_ssq, s4_rms, s4_rrms, s4_xn = sems4("ssq rms rrms xn")

        @b4.sync
        def _(sp):
            sp.wait_ge(s4_zrow, 1)
            sp.dma_start(y_dram[NB_MIN * P:].rearrange("(p b) (a n) -> p (b a) n", p=P, n=256),
                         zrow.unsqueeze(1).broadcast_to([P, (NB - NB_MIN) * D // 256, 256])).then_inc(s4_fill, 16)
            for k in range(KT):
                sp.dma_start(wo[k], w_out[0, k * P:(k + 1) * P, :]).then_inc(s4_wo, 16)
            sp.wait_ge(s4_o, 2 * 16)
            sp.wait_ge(s4_S, 2 * STEPS)
            sp.dma_start(gate1, drow(gate_dram[0:1, :])).then_inc(s4_g1, 16)
            sp.dma_start(xr, x.rearrange("a (t p) n -> p (a t) n", p=P)).then_inc(s4_x, 16)
            sp.wait_ge(s4_fill, 16)

        @b4.gpsimd
        def _(pool):
            nc.gpsimd.memset(zrow, 0.0).then_inc(s4_zrow, 1)
            nc.gpsimd.memset(S_, 0.0).then_inc(s4_zero, 1)
            for i in range(STEPS):
                for d in range(2):
                    t, c_ = chunk_of(i, d)
                    r = slice(64 * c_, 64 * c_ + 64)
                    rd = slice(64 * d, 64 * d + 64)
                    n = 2 * i + d
                    if n:
                        pool.wait_ge(s4_kd, n)
                    if i >= 2:
                        pool.wait_ge(s4_up, 2 * (i - 2) + d + 1)
                        if d == 0:
                            pool.wait_ge(s4_up, 2 * (i - 2) + 2)
                    nc.gpsimd.tensor_tensor(kd[r, i % 2], tok[r, t, 1], heads(ekd[r, t, d]), ALU.mult).then_inc(s4_kd, 1)
                if i:
                    pool.wait_ge(s4_S, 2 * i)
                else:
                    pool.wait_ge(s4_zero, 1)
                pool.wait_ge(s4_kd, 2 * i + 2)
                for d in range(2):
                    t, c_ = chunk_of(i, d)
                    rd = slice(64 * d, 64 * d + 64)
                    if d:
                        pool.wait_ge(s4_Sg, 2 * i + 1)
                    nc.gpsimd.tensor_tensor(Sg[rd], S_[rd, i % 2], heads(glb[rd, c_, t]), ALU.mult).then_inc(s4_Sg, 1)

        @b4.scalar
        def _(act):
            for i in range(4, STEPS):
                for d in range(2):
                    t, c_ = chunk_of(i, d)
                    r = slice(64 * c_, 64 * c_ + 64)
                    n = 2 * (i - 4) + d
                    act.wait_ge(s4_o1, n + 1)
                    if n >= 4:
                        act.wait_ge(s4_o, n - 2 if d == 0 else n - 3)
                    nc.scalar.activation(o1s[r, i % 2].rearrange("p h n -> p (h n)"), psum[r, 4 + d, 0:256], ACT.Copy
                                         ).then_inc(s4_o1c, 1)
            act.wait_ge(s4_oss, 1)
            nc.scalar.activation(oss, oss, ACT.Sqrt, bias=epst, scale=1.0 / HD).then_inc(s4_std, 1)
            for n in range(4):
                m, hh = divmod(n, 2)
                act.wait_ge(s4_yt, n + 1)
                nc.scalar.activation(gdnT[:, m, hh * 512:(hh + 1) * 512], psum[:, n, :], ACT.Copy).then_inc(s4_yv, 1)
            for t in range(NT):
                act.wait_ge(s4_res, 2 * t + 2)
                if t:
                    act.wait_ge(s4_ssq, t)
                nc.scalar.activation(psum[:, 0:2, :].rearrange("p a n -> p (a n)"), x1[:, t], ACT.Square,
                                     accum_out=ssq[:, t:t + 1]).then_inc(s4_ssq, 1)
                act.wait_ge(s4_ssq, t + 1)
                nc.scalar.activation(rstd[:, t:t + 1], ssq[:, t:t + 1], ACT.Sqrt, bias=epst, scale=1.0 / D
                                     ).then_inc(s4_rms, 1)

        @b4.vector
        def _(dve):
            link = [0]

            def chain(ins):
                link[0] += 1
                bump(dve, s4_v, ins, link[0])

            for i in range(STEPS):
                for d in range(2):
                    t, c_ = chunk_of(i, d)
                    r = slice(64 * c_, 64 * c_ + 64)
                    dve.wait_ge(s4_wS, 2 * i + d + 1)
                    if i >= 2 and d == 0:
                        dve.wait_ge(s4_up, 2 * i - 2)
                        if i >= 6:
                            dve.wait_ge(s4_o2, 2 * (i - 6) + 2)
                    nc.vector.tensor_tensor(vn[r, i % 2], u_all[r, t, d],
                                            psum[r, d, 0:256].rearrange("p (h n) -> p h n", h=NH), ALU.subtract
                                            ).then_inc(s4_vn, 1)
                for d in range(2):
                    t, c_ = chunk_of(i, d)
                    rd = slice(64 * d, 64 * d + 64)
                    dve.wait_ge(s4_up, 2 * i + d + 1)
                    dve.wait_ge(s4_Sg, 2 * i + d + 1)
                    if i >= 1 and d == 0:
                        dve.wait_ge(s4_Sg, 2 * i)
                        if i >= 5:
                            dve.wait_ge(s4_o1, 2 * (i - 5) + 2)
                    nc.vector.tensor_tensor(S_[rd, (i + 1) % 2], Sg[rd],
                                            psum[rd, 2 + c_, 0:256].rearrange("p (h n) -> p h n", h=NH), ALU.add
                                            ).then_inc(s4_S, 1)
                if i >= 4:
                    for d in range(2):
                        t, c_ = chunk_of(i, d)
                        r = slice(64 * c_, 64 * c_ + 64)
                        n = 2 * (i - 4) + d
                        dve.wait_ge(s4_o1c, n + 1)
                        dve.wait_ge(s4_o2, n + 1)
                        nc.vector.tensor_tensor(o_f[r, d, t - NCT], o1s[r, i % 2].rearrange("p h n -> p (h n)"),
                                                psum[r, 6 + c_, 0:256], ALU.add).then_inc(s4_o, 1)
            dve.wait_ge(s4_o, 2 * 16)
            of = otok.rearrange("p t h n -> p t (h n)")
            chain(nc.vector.tensor_tensor(of, o_f[:, 0], o_f[:, 1], ALU.add))
            chain(nc.vector.tensor_tensor(osq, otok, otok, ALU.mult))
            nc.vector.tensor_reduce(oss, osq.rearrange("p t h n -> p (t h) n"), AX.X, ALU.add).then_inc(s4_oss, 1)
            dve.wait_ge(s4_std, 1)
            chain(nc.vector.reciprocal(oss, oss))
            ov = otok.rearrange("p t h n -> p (t h) n")
            chain(nc.vector.tensor_tensor(ov, ov, oss.unsqueeze(2).broadcast_to([P, NT * NH, HD]), ALU.mult))
            chain(nc.vector.tensor_tensor(ov, ov, gnr.unsqueeze(1).broadcast_to([P, NT * NH, HD]), ALU.mult))
            nc.vector.tensor_tensor(of, of, zs, ALU.mult).then_inc(s4_y, 1)
            dve.wait_ge(s4_g1, 16)
            dve.wait_ge(s4_x, 16)
            def normalise(t):
                dve.wait_ge(s4_rms, t + 1)
                nc.vector.reciprocal(rstd[:, t:t + 1], rstd[:, t:t + 1]).then_inc(s4_rrms, 1)
                dve.wait_ge(s4_rrms, t + 1)
                if t == 4:
                    dve.wait_ge(s4_yt, 4)
                nc.vector.tensor_scalar(xn[t], x1[:, t], rstd[:, t:t + 1], None, ALU.mult).then_inc(s4_xn, 1)

            for n in range(2 * NT):
                t, hh = divmod(n, 2)
                cols = slice(hh * 512, (hh + 1) * 512)
                dve.wait_ge(s4_mm, n + 1)
                nc.vector.tensor_tensor(x1[:, t, cols], psum[:, 4 + n % 4, :], gate1[:, cols], ALU.mult).then_inc(s4_ev, 1)
                dve.wait_ge(s4_ev, n + 1)
                nc.vector.tensor_tensor(x1[:, t, cols], x1[:, t, cols], xr[:, t, cols], ALU.add).then_inc(s4_res, 1)
                if hh and t:
                    normalise(t - 1)
            normalise(NT - 1)

        @b4.tensor
        def _(pe):
            pe.wait_ge(s4_zero, 1)
            for i in range(STEPS):
                for d in range(2):
                    t, c_ = chunk_of(i, d)
                    r, rd = slice(64 * c_, 64 * c_ + 64), slice(64 * d, 64 * d + 64)
                    if i:
                        pe.wait_ge(s4_S, 2 * (i - 1) + d + 1)
                        pe.wait_ge(s4_vn, 2 * (i - 1) + d + 1)
                    for h in range(NH):
                        last = nc.tensor.matmul(psum[r, d, h * HD:(h + 1) * HD], wT_all[rd, t, h, r], S_[rd, i % 2, h],
                                                start=True, stop=True)
                    last.then_inc(s4_wS, 1)
                if i >= 4:
                    for d in range(2):
                        t, c_ = chunk_of(i, d)
                        r, rd = slice(64 * c_, 64 * c_ + 64), slice(64 * d, 64 * d + 64)
                        if i >= 5:
                            pe.wait_ge(s4_o1c, 2 * (i - 5) + d + 1)
                        for h in range(NH):
                            last = nc.tensor.matmul(psum[r, 4 + d, h * HD:(h + 1) * HD], qgT_all[rd, t - NCT, h, r],
                                                    S_[rd, i % 2, h], start=True, stop=True)
                        last.then_inc(s4_o1, 1)
                for d in range(2):
                    t, c_ = chunk_of(i, d)
                    r, rd = slice(64 * c_, 64 * c_ + 64), slice(64 * d, 64 * d + 64)
                    pe.wait_ge(s4_kd, 2 * i + d + 1)
                    pe.wait_ge(s4_vn, 2 * i + d + 1)
                    if i:
                        pe.wait_ge(s4_S, 2 * i)
                    for h in range(NH):
                        last = nc.tensor.matmul(psum[rd, 2 + c_, h * HD:(h + 1) * HD], kd[r, i % 2, h], vn[r, i % 2, h],
                                                start=True, stop=True)
                    last.then_inc(s4_up, 1)
                if i >= 4:
                    for d in range(2):
                        t, c_ = chunk_of(i, d)
                        r = slice(64 * c_, 64 * c_ + 64)
                        if i >= 5:
                            pe.wait_ge(s4_o, 2 * (i - 5) + 2)
                        for h in range(NH):
                            last = nc.tensor.matmul(psum[r, 6 + c_, h * HD:(h + 1) * HD],
                                                    pT_all[r, t - NCT, d, h * HD:(h + 1) * HD], vn[r, i % 2, h],
                                                    start=True, stop=True)
                        last.then_inc(s4_o2, 1)
            mix = [convT[:, 0], convT[:, 1], gdnT[:, 0], gdnT[:, 1]] + [attnT[:, k] for k in range(4)]
            early_k, late_k = (0, 1, 4, 5, 6, 7), (2, 3)

            def project(n, ks):
                t, hh = divmod(n, 2)
                for k in ks:
                    last = nc.tensor.matmul(psum[:, 4 + n % 4, :], mix[k][:, t * P:(t + 1) * P],
                                            wo[k][:, hh * 512:(hh + 1) * 512], start=k == 0, stop=k == late_k[-1])
                return last

            pe.wait_ge(s4_wo, 16 * KT)
            pe.wait_ge(s4_o, 2 * 16)
            for n in range(4):
                project(n, early_k)
            pe.wait_ge(s4_y, 1)
            for n in range(4):
                m, hh = divmod(n, 2)
                for t in range(4):
                    last = nc.tensor.transpose(psum[:, n, t * P:(t + 1) * P],
                                               otok[:, hh * 4 + t, 2 * m:2 * m + 2].rearrange("p h n -> p (h n)"), ident)
                last.then_inc(s4_yt, 1)
            pe.wait_ge(s4_yv, 4)
            for n in range(2 * NT):
                if n >= 4:
                    pe.wait_ge(s4_ev, n - 3)
                    project(n, early_k)
                project(n, late_k).then_inc(s4_mm, 1)

        fourth.close()
        retire_semaphores()

        xhat_dram = nc.dram_tensor("xhat", (L, D), F32).ap()
        map_dram = nc.dram_tensor("slot_token", (NB * P, 1), F32).ap()

        h2T = at(101, 2, KT, 512)
        wr = at(97, KT, NG + NE)
        lgT = at(98.5, 2, 512)
        lg = at(162, NT, NG + NE)
        gpad, gmax = at(164, NT, 8), at(164.25, NT, 8)
        gidx, gidf = at(164.5, NT, 8, dt=U32), at(164.75, NT, 1)
        gexp, gsum = at(165, NT, NG), at(165.25, NT)
        ge = at(165.5, NT)
        inG, le = at(166, NT, NE), at(167, NT, NE)
        m1, i1 = at(168, NT, 8), at(168.25, NT, 8, dt=U32)
        m2, i2 = at(168.5, NT, 8), at(168.75, NT, 8, dt=U32)
        sel1, sel2, selS = at(169, NT, NE), at(170, NT, NE), at(171, NT, NE)
        before = at(172, NT + 1, NE)
        rank = at(174, NT, NE)
        cnt, nbs, bend, bst, zer = at(175, NE), at(177, NE), at(177.25, NE), at(177.5, NE), at(177.75, NE)
        more = at(176, NE, 8)
        ended = at(178, NB, NE)
        blkf, blk_e = at(184, NB), at(184.25, NB, dt=I32)
        w1, w2 = at(184.5, NT), at(184.625, NT)
        slf1, slf2 = at(184.75, NT), at(184.875, NT)
        slot1, slot2 = at(185, NT, dt=I32), at(185.125, NT, dt=I32)
        pairf, pairsum, pairs = at(185.25, 24), at(185.5, 1), at(185.625, 1, dt=I32)
        e_row, g_row, j_row, b_row, pair_row = at(186, NE), at(186.25, NE), at(186.5, 8), at(186.75, NB), at(187.25, 24)
        tok_id = at(187.5, NT)
        rbias = at(188, NG + NE)
        mapT, slot_tok = at(188.5, P), at(189.5, NB, dt=I32)
        early, ones5, zero5 = at(190, P), at(190.5, P), at(191, P)
        i1f, i2f, e2, wsum = at(191.5, NT, 1), at(191.625, NT, 1), at(191.75, NT), at(191.875, NT)

        fifth = ExitStack()
        b5 = fifth.enter_context(nc.Block())

        def sems5(names):
            return (sem("s5_" + n) for n in names.split())

        s5_wr, s5_early, s5_iota, s5_zero, s5_map, s5_mapT = sems5("wr early iota zero map mapT")
        s5_v, s5_xst, s5_t, s5_ta, s5_td = sems5("v xst t ta td")
        s5_lt, s5_ltc, s5_l, s5_le, s5_exp, s5_e2 = sems5("lt ltc l le exp e2")
        s5_sel, s5_rank, s5_slot, s5_tr, s5_idx, s5_ord = sems5("sel rank slot tr idx ord")
        s5_blk = sem("s5_blk")
        FT = FE // P
        gate_w = [at(0, KT, FE), at(16, KT, FE)]
        up_w = [at(32, KT, FE), at(48, KT, FE)]
        down_w = [at(97, FT, D), at(113, FT, D)]
        s6_gate, s6_up, s6_down = ([sem(f"s6_{name}{i}") for i in range(2)] for name in ("gate", "up", "down"))
        s6_G, s6_U, s6_D = sem("s6_G"), sem("s6_U"), sem("s6_D")
        gw = expert_w_gate.rearrange("a e (k p) f -> p (a e) k f", p=P)
        uw = expert_w_up.rearrange("a e (k p) f -> p (a e) k f", p=P)
        dw = expert_w_down.rearrange("a e (k p) f -> p (a e) k f", p=P)

        def weights(sp, b, s, done, which=(0, 1, 2)):
            ex = sp.value_load(blk_e[0:1, bass.ds(b, 1)], min_val=0, max_val=NE - 1)
            for i in which:
                ring_, w, ready, used = ((gate_w, gw, s6_gate, s6_G), (up_w, uw, s6_up, s6_U),
                                         (down_w, dw, s6_down, s6_D))[i]
                if done is not None and not (isinstance(done, int) and done == 0):
                    sp.wait_ge(used, done)
                sp.dma_start(ring_[s], w[:, bass.ds(ex, 1)].rearrange("p e k f -> p (e k) f")
                             ).then_inc(ready[s], 16)

        @b5.sync
        def _(sp):
            sp.dma_start(wr[:, :, 0:NG], router_group_w.rearrange("a (k p) n -> p (a k) n", p=P)).then_inc(s5_wr, 16)
            sp.dma_start(wr[:, :, NG:], router_expert_w.rearrange("a (k p) n -> p (a k) n", p=P)).then_inc(s5_wr, 16)
            sp.dma_start(rbias[:, 0:NG], drow(router_group_b)).then_inc(s5_wr, 16)
            sp.dma_start(rbias[:, NG:], drow(router_expert_b)).then_inc(s5_wr, 16)
            sp.dma_start(early, cst[:, M_EARLY * P:(M_EARLY + 1) * P]).then_inc(s5_early, 16)
            sp.wait_ge(s5_iota, 1)
            sp.dma_start(map_dram.rearrange("(b s) a -> b (s a)", b=NB), zero5[0:NB]).then_inc(s5_zero, 16)
            for t in range(NT):
                sp.dma_start(xhat_dram[t * P:(t + 1) * P, :], xn[t]).then_inc(s5_xst, 16)
            sp.wait_ge(s5_xst, 16 * NT)
            sp.wait_ge(s5_blk, 1)
            weights(sp, 0, 0, None, (0,))
            sp.wait_ge(s5_map, 16 * 2 * NT)
            sp.dma_start(mapT[0:NB], map_dram.rearrange("(b s) a -> b (s a)", b=NB)).then_inc(s5_mapT, 16)

        @b5.gpsimd
        def _(pool):
            e = nc.gpsimd
            e.memset(zero5, 0.0)
            e.memset(zer, 0.0)
            e.memset(ones5, 1.0)
            e.memset(gpad, NEG)
            f = dict(allow_small_or_imprecise_dtypes=True)
            e.iota(e_row, [[1, NE]], base=0, channel_multiplier=0, **f)
            e.iota(g_row, [[1, NG], [0, EPG]], base=0, channel_multiplier=0, **f)
            e.iota(j_row, [[P, 8]], base=0, channel_multiplier=0, **f)
            e.iota(b_row, [[1, NB]], base=0, channel_multiplier=0, **f)
            e.iota(pair_row, [[2, 24]], base=1, channel_multiplier=0, **f)
            e.iota(tok_id, [[P, NT]], base=0, channel_multiplier=1, **f).then_inc(s5_iota, 1)
            pool.wait_ge(s5_iota, 1)
            pool.wait_ge(s5_zero, 16)
            for n, slot in enumerate((slot1, slot2)):
                pool.wait_ge(s5_slot, n + 1)
                for t in range(NT):
                    e.indirect_dma_start(map_dram[:, :], bass.IndirectOffsetOnAxis(ap=slot[:, t:t + 1], axis=0),
                                         tok_id[:, t:t + 1], None).then_inc(s5_map, 16)

        @b5.scalar
        def _(act):
            for n in range(2 * KT):
                hh, k = divmod(n, KT)
                if k % 2 == 0:
                    act.wait_ge(s5_t, n + 1)
                    nc.scalar.activation(h2T[:, hh, k], psum[:, n % 4, :], ACT.Identity, bias=colB2[:, k:k + 1],
                                         scale=colA2[:, k:k + 1]).then_inc(s5_ta, 1)
            for hh in range(2):
                act.wait_ge(s5_lt, hh + 1)
                nc.scalar.activation(lgT[0:NG + NE, hh], psum[0:NG + NE, 4 + hh, :], ACT.Copy).then_inc(s5_ltc, 1)
            act.wait_ge(s5_le, 1)
            nc.scalar.activation(gexp, gexp, ACT.Exp).then_inc(s5_exp, 1)
            act.wait_ge(s5_le, 2)
            nc.scalar.activation(e2, e2, ACT.Exp).then_inc(s5_e2, 1)

        @b5.vector
        def _(dve):
            e = nc.vector
            link = [0]

            def chain(ins):
                link[0] += 1
                bump(dve, s5_v, ins, link[0])

            for n in range(2 * KT):
                hh, k = divmod(n, KT)
                if k % 2:
                    dve.wait_ge(s5_t, n + 1)
                    e.tensor_scalar(h2T[:, hh, k], psum[:, n % 4, :], colA2[:, k:k + 1], colB2[:, k:k + 1],
                                    ALU.mult, ALU.add).then_inc(s5_td, 1)
            dve.wait_ge(s5_l, 1)
            dve.wait_ge(s5_wr, 64)
            dve.wait_ge(s5_iota, 1)
            ne = NG + NE
            chain(e.tensor_tensor(lg, psum[:, 6, 0:NT * ne].rearrange("p (t n) -> p t n", t=NT),
                                  rbias.unsqueeze(1).broadcast_to([P, NT, ne]), ALU.add))
            chain(e.tensor_copy(gpad[:, :, 0:NG], lg[:, :, 0:NG]))
            for t in range(NT):
                last = e.max(gmax[:, t], gpad[:, t])
            chain(last)
            for t in range(NT):
                last = e.max_index(gidx[:, t], gmax[:, t], gpad[:, t])
            last.then_inc(s5_ord, 1)
            e.tensor_tensor(gexp, lg[:, :, 0:NG], gmax[:, :, 0:1].broadcast_to([P, NT, NG]), ALU.subtract
                            ).then_inc(s5_le, 1)
            dve.wait_ge(s5_ord, 1)
            chain(e.tensor_copy(gidf, gidx[:, :, 0:1]))
            grow = g_row.unsqueeze(1).broadcast_to([P, NT, NE])
            erow = e_row.unsqueeze(1).broadcast_to([P, NT, NE])
            chain(e.tensor_tensor(inG, grow, gidf.broadcast_to([P, NT, NE]), ALU.is_equal))
            chain(e.tensor_scalar(inG, inG, -NEG, NEG, ALU.mult, ALU.add))
            chain(e.tensor_tensor(le, lg[:, :, NG:], inG, ALU.add))
            for m, i, f_, sel in ((m1, i1, i1f, sel1), (m2, i2, i2f, sel2)):
                for t in range(NT):
                    last = e.max(m[:, t], le[:, t])
                chain(last)
                for t in range(NT):
                    last = e.max_index(i[:, t], m[:, t], le[:, t])
                chain(last)
                chain(e.tensor_copy(f_, i[:, :, 0:1]))
                chain(e.tensor_tensor(sel, erow, f_.broadcast_to([P, NT, NE]), ALU.is_equal))
                if sel is sel1:
                    chain(e.scalar_tensor_tensor(le, sel, NEG, le, ALU.mult, ALU.add))
            m1v, m2v = m1[:, :, 0], m2[:, :, 0]
            e.tensor_tensor(e2, m2v, m1v, ALU.subtract).then_inc(s5_le, 1)
            chain(e.tensor_tensor(selS, sel1, sel2, ALU.add))
            chain(e.tensor_copy(before[:, 0], zer))
            for t in range(NT):
                chain(e.tensor_tensor(before[:, t + 1], before[:, t], selS[:, t], ALU.add))
            e.tensor_copy(gidf[:, 0:1, 0], zer[:, 0:1]).then_inc(s5_sel, 1)
            dve.wait_ge(s5_exp, 1)
            chain(e.tensor_reduce(gsum, gexp, AX.X, ALU.add))
            dve.wait_ge(s5_e2, 1)
            chain(e.tensor_scalar(wsum, e2, 1.0, None, ALU.add))
            chain(e.tensor_tensor(wsum, wsum, gsum, ALU.mult))
            chain(e.reciprocal(w1, wsum))
            chain(e.tensor_tensor(w2, w1, e2, ALU.mult))
            dve.wait_ge(s5_rank, 1)
            chain(e.tensor_copy(cnt, psum[:, 7, 256:256 + NE]))
            chain(e.tensor_tensor(more, cnt.unsqueeze(2).broadcast_to([P, NE, 8]),
                                  j_row.unsqueeze(1).broadcast_to([P, NE, 8]), ALU.is_gt))
            chain(e.tensor_reduce(nbs, more, AX.X, ALU.add))
            chain(e.tensor_tensor_scan(bend, nbs, zer, 0.0, ALU.add, ALU.add))
            chain(e.tensor_tensor(bst, bend, nbs, ALU.subtract))
            chain(e.tensor_scalar(bst, bst, float(P), None, ALU.mult))
            chain(e.tensor_tensor(rank, psum[:, 7, 0:NT * NE].rearrange("p (t n) -> p t n", t=NT),
                                  bst.unsqueeze(1).broadcast_to([P, NT, NE]), ALU.add))
            for sel, sf, slot in ((sel1, slf1, slot1), (sel2, slf2, slot2)):
                chain(e.tensor_tensor(sel, sel, rank, ALU.mult))
                chain(e.tensor_reduce(sf, sel, AX.X, ALU.add))
                e.tensor_copy(slot, sf).then_inc(s5_slot, 1)
            chain(e.tensor_tensor(ended, bend.unsqueeze(1).broadcast_to([P, NB, NE]),
                                  b_row.unsqueeze(2).broadcast_to([P, NB, NE]), ALU.is_le))
            chain(e.tensor_reduce(blkf, ended, AX.X, ALU.add))
            chain(e.tensor_scalar(blkf, blkf, float(NE - 1), None, ALU.min))
            e.tensor_copy(blk_e, blkf).then_inc(s5_blk, 1)
            chain(e.tensor_tensor(pairf, bend[:, NE - 1:NE].broadcast_to([P, 24]), pair_row, ALU.is_gt))
            chain(e.tensor_reduce(pairsum, pairf, AX.X, ALU.add))
            chain(e.tensor_copy(pairs, pairsum))
            dve.wait_ge(s5_tr, 1)
            e.tensor_copy(slot_tok, psum[:, 6, 0:NB]).then_inc(s5_idx, 1)

        @b5.tensor
        def _(pe):
            for n in range(2 * KT):
                hh, k = divmod(n, KT)
                if n >= 4:
                    if n % 2 == 0:
                        pe.wait_ge(s5_ta, n // 2 - 1)
                    else:
                        pe.wait_ge(s5_td, n // 2 - 1)
                for t in range(4):
                    last = nc.tensor.transpose(psum[:, n % 4, t * P:(t + 1) * P],
                                               xn[4 * hh + t][:, k * P:(k + 1) * P], ident)
                last.then_inc(s5_t, 1)
            pe.wait_ge(s5_wr, 64)
            for hh in range(2):
                pe.wait_ge(s5_ta, 4 * (hh + 1))
                pe.wait_ge(s5_td, 4 * (hh + 1))
                for k in range(KT):
                    last = nc.tensor.matmul(psum[0:NG + NE, 4 + hh, :], wr[:, k], h2T[:, hh, k],
                                            start=k == 0, stop=k == KT - 1)
                last.then_inc(s5_lt, 1)
            ne = NG + NE
            for t in range(NT):
                pe.wait_ge(s5_ltc, t // 4 + 1)
                last = nc.tensor.matmul(psum[:, 6, t * ne:(t + 1) * ne],
                                        lgT[0:ne, t // 4, (t % 4) * P:(t % 4 + 1) * P], ident[0:ne, 0:ne],
                                        start=True, stop=True)
            last.then_inc(s5_l, 1)
            pe.wait_ge(s5_sel, 1)
            pe.wait_ge(s5_early, 16)
            pe.wait_ge(s5_iota, 1)
            nc.tensor.matmul(psum[:, 7, 0:NT * NE], early, selS.rearrange("p t n -> p (t n)"), start=True, stop=False)
            nc.tensor.matmul(psum[:, 7, 0:NT * NE], ones5, before[:, 0:NT].rearrange("p t n -> p (t n)"),
                             start=False, stop=True)
            nc.tensor.matmul(psum[:, 7, 256:256 + NE], ones5, before[:, NT], start=True, stop=True
                             ).then_inc(s5_rank, 1)
            pe.wait_ge(s5_mapT, 16)
            nc.tensor.transpose(psum[:, 6, 0:NB], mapT[0:NB, :], ident[0:NB, 0:NB]).then_inc(s5_tr, 1)

        fifth.close()

        xg = [at(129, D), at(133, D)]
        xgT = [at(137, KT, P), at(141, KT, P)]
        hid = [at(145, FT, P), at(147, FT, P)]
        sg = [at(149, FT, P), at(151, FT, P)]
        ye = [at(153, D), at(157, D)]
        col = [at(161, 1, dt=I32), at(161.25, 1, dt=I32)]

        idle = at(161.5, 1)
        PAIRS_MIN, PAIRS = NB_MIN // 2, NB // 2 - 1
        sixth = ExitStack()
        b6 = sixth.enter_context(nc.Block())

        def sems6(names):
            return (sem("s6_" + n) for n in names.split())

        def slots6(name):
            return [sem(f"s6_{name}{i}") for i in range(2)]

        s6_xg, s6_yst = slots6("xg"), slots6("yst")
        s6_col, s6_X = sems6("col X")
        s6_sg, s6_h, s6_xA, s6_xD, s6_yA, s6_yD = sems6("sg h xA xD yA yD")

        def first(count):
            return count is None or (isinstance(count, int) and count == 0)

        def pair_count(eng):
            return eng.value_load(pairs[0:1, 0:1], min_val=PAIRS_MIN, max_val=PAIRS)

        @b6.sync
        def _(sp):
            n = pair_count(sp)
            weights(sp, 0, 0, None, (1, 2))

            def pair(i):
                weights(sp, i * 2 + 1, 1, i * 2)
                weights(sp, i * 2 + 2, 0, i * 2 + 1)

            pair(0)
            with sp.Fori(1, n) as i:
                pair(i)

        @b6.gpsimd
        def _(pool):
            def gather(b, s, used, before_):
                if not first(before_):
                    pool.wait_ge(s6_xg[s], before_)
                nc.gpsimd.tensor_copy(col[s], slot_tok[:, bass.ds(b, 1)]).then_inc(s6_col, 1)
                pool.wait_ge(s6_col, b + 1)
                if not first(used):
                    pool.wait_ge(s6_X, used)
                    nc.gpsimd.tensor_tensor(idle, idle, idle, ALU.add)
                nc.gpsimd.indirect_dma_start(xg[s], None, xhat_dram[:, :],
                                             bass.IndirectOffsetOnAxis(ap=col[s], axis=0)).then_inc(s6_xg[s], 16)

            n = pair_count(pool)
            nc.gpsimd.memset(idle, 0.0)
            gather(0, 0, None, None)
            gather(1, 1, None, None)
            def pair(i):
                gather(i * 2 + 2, 0, i * 2 + 1, (i + 1) * 16)
                gather(i * 2 + 3, 1, i * 2 + 2, (i + 1) * 16)

            pair(0)
            with pool.Fori(1, n) as i:
                pair(i)
            pool.wait_ge(s6_xg[0], (n + 1) * 16)
            pool.wait_ge(s6_xg[1], (n + 1) * 16)
            pool.wait_ge(s6_yst[0], (n + 1) * 16)
            pool.wait_ge(s6_yst[1], n * 16)

        @b6.scalar
        def _(act):
            def tokens(b, s):
                act.wait_ge(s6_X, b + 1)
                for k in range(4):
                    last = nc.scalar.activation(xgT[s][:, k], psum[:, 4, k * P:(k + 1) * P], ACT.Identity,
                                                bias=colB2[:, k:k + 1], scale=colA2[:, k:k + 1])
                last.then_inc(s6_xA, 1)

            def gate(b, s, h_used):
                act.wait_ge(s6_G, b + 1)
                if not first(h_used):
                    act.wait_ge(s6_h, h_used)
                nc.scalar.activation(sg[s], psum[:, 2 * s, :].rearrange("p (m n) -> p m n", m=FT), ACT.Silu
                                     ).then_inc(s6_sg, 1)

            def result(b, s, stored):
                act.wait_ge(s6_D, b + 1)
                if not first(stored):
                    act.wait_ge(s6_yst[s], stored)
                nc.scalar.activation(ye[s][:, 0:512], psum[:, 6, :], ACT.Copy).then_inc(s6_yA, 1)
                act.wait_ge(s6_yA, b + 1)
                act.wait_ge(s6_yD, b + 1)
                act.dma_start(y_dram.rearrange("(b p) n -> b p n", p=P)[bass.ds(b, 1)].rearrange("b p n -> (b p) n"),
                              ye[s]).then_inc(s6_yst[s], 16)

            n = pair_count(act)
            tokens(0, 0)
            gate(0, 0, None)
            tokens(1, 1)
            def pair(i):
                gate(i * 2 + 1, 1, i * 2)
                tokens(i * 2 + 2, 0)
                result(i * 2, 0, i * 16)
                gate(i * 2 + 2, 0, i * 2 + 1)
                tokens(i * 2 + 3, 1)
                result(i * 2 + 1, 1, i * 16)

            pair(0)
            with act.Fori(1, n) as i:
                pair(i)
            result(n * 2, 0, n * 16)

        @b6.vector
        def _(dve):
            def tokens(b, s):
                dve.wait_ge(s6_X, b + 1)
                for k in range(4, 8):
                    last = nc.vector.tensor_scalar(xgT[s][:, k], psum[:, 5, (k - 4) * P:(k - 3) * P],
                                                   colA2[:, k:k + 1], colB2[:, k:k + 1], ALU.mult, ALU.add)
                last.then_inc(s6_xD, 1)

            def hidden(b, s, d_used):
                dve.wait_ge(s6_U, b + 1)
                dve.wait_ge(s6_sg, b + 1)
                if not first(d_used):
                    dve.wait_ge(s6_D, d_used)
                nc.vector.tensor_tensor(hid[s], sg[s], psum[:, 2 * s + 1, :].rearrange("p (m n) -> p m n", m=FT),
                                        ALU.mult).then_inc(s6_h, 1)

            def result(b, s, stored):
                dve.wait_ge(s6_D, b + 1)
                if not first(stored):
                    dve.wait_ge(s6_yst[s], stored)
                nc.vector.tensor_copy(ye[s][:, 512:], psum[:, 7, :]).then_inc(s6_yD, 1)

            n = pair_count(dve)
            tokens(0, 0)
            hidden(0, 0, None)
            tokens(1, 1)
            def pair(i):
                hidden(i * 2 + 1, 1, i * 2)
                tokens(i * 2 + 2, 0)
                result(i * 2, 0, i * 16)
                hidden(i * 2 + 2, 0, i * 2 + 1)
                tokens(i * 2 + 3, 1)
                result(i * 2 + 1, 1, i * 16)

            pair(0)
            with dve.Fori(1, n) as i:
                pair(i)
            result(n * 2, 0, n * 16)

        @b6.tensor
        def _(pe):
            def tokens(b, s, landed, free):
                pe.wait_ge(s6_xg[s], landed)
                if not first(free):
                    pe.wait_ge(s6_xA, free)
                    pe.wait_ge(s6_xD, free)
                for k in range(KT):
                    last = nc.tensor.transpose(psum[:, 4 + k // 4, (k % 4) * P:(k % 4 + 1) * P],
                                               xg[s][:, k * P:(k + 1) * P], ident)
                last.then_inc(s6_X, 1)

            def gate_up(b, s, landed, used):
                pe.wait_ge(s6_xA, b + 1)
                pe.wait_ge(s6_xD, b + 1)
                for w, ready, done, bank, taken in ((gate_w[s], s6_gate[s], s6_G, 2 * s, s6_sg),
                                                    (up_w[s], s6_up[s], s6_U, 2 * s + 1, s6_h)):
                    pe.wait_ge(ready, landed)
                    if not first(used):
                        pe.wait_ge(taken, used)
                    for m in range(FT):
                        for k in range(KT):
                            last = nc.tensor.matmul(psum[:, bank, m * P:(m + 1) * P], w[:, k, m * P:(m + 1) * P],
                                                    xgT[s][:, k], start=k == 0, stop=k == KT - 1)
                    last.then_inc(done, 1)

            def down(b, s, landed, used):
                pe.wait_ge(s6_down[s], landed)
                pe.wait_ge(s6_h, b + 1)
                if not first(used):
                    pe.wait_ge(s6_yA, used)
                    pe.wait_ge(s6_yD, used)
                for hh in range(2):
                    for k in range(FT):
                        last = nc.tensor.matmul(psum[:, 6 + hh, :], hid[s][:, k], down_w[s][:, k, hh * 512:(hh + 1) * 512],
                                                start=k == 0, stop=k == FT - 1)
                last.then_inc(s6_D, 1)

            n = pair_count(pe)
            tokens(0, 0, 16, None)
            gate_up(0, 0, 16, None)
            tokens(1, 1, 16, 1)
            def pair(i):
                gate_up(i * 2 + 1, 1, (i + 1) * 16, i * 2)
                tokens(i * 2 + 2, 0, (i + 2) * 16, i * 2 + 2)
                down(i * 2, 0, (i + 1) * 16, i * 2)
                gate_up(i * 2 + 2, 0, (i + 2) * 16, i * 2 + 1)
                tokens(i * 2 + 3, 1, (i + 2) * 16, i * 2 + 3)
                down(i * 2 + 1, 1, (i + 1) * 16, i * 2 + 1)

            pair(0)
            with pe.Fori(1, n) as i:
                pair(i)
            down(n * 2, 0, (n + 1) * 16, n * 2)

        sixth.close()

        y1, y2 = at(0, NT, D), at(32, NT, D)
        gate2, gainF = at(97, D), at(101, D)
        yw = at(105, 2, D)
        sq7 = at(113, D)
        yo = at(117, NT, D)

        seventh = ExitStack()
        b7 = seventh.enter_context(nc.Block())
        s7_y = [sem(f"s7_y{t}") for t in range(NT)]
        s7_row, s7_w, s7_sum, s7_gated, s7_x2, s7_ssq, s7_std, s7_rstd, s7_out, s7_st = (
            sem("s7_" + n) for n in "row w sum gated x2 ssq std rstd out st".split())

        @b7.gpsimd
        def _(pool):
            ahead = 3
            for t in range(NT + ahead):
                if t < NT:
                    for dst, slot in ((y1, slot1), (y2, slot2)):
                        nc.gpsimd.indirect_dma_start(dst[:, t], None, y_dram[:, :],
                                                     bass.IndirectOffsetOnAxis(ap=slot[:, t:t + 1], axis=0)
                                                     ).then_inc(s7_y[t], 16)
                if t >= ahead:
                    u = t - ahead
                    if u == 0:
                        pool.wait_ge(s7_row, 32)
                    pool.wait_ge(s7_sum, u + 1)
                    nc.gpsimd.tensor_tensor(y2[:, u], y2[:, u], gate2, ALU.mult).then_inc(s7_gated, 1)

        @b7.sync
        def _(sp):
            sp.dma_start(gate2, drow(gate_dram[1:2, :])).then_inc(s7_row, 16)
            sp.dma_start(gainF, final_norm_g.partition_broadcast(P)).then_inc(s7_row, 16)
            for t in range(NT):
                sp.wait_ge(s7_out, t + 1)
                sp.dma_start(out[0, t * P:(t + 1) * P, :], yo[:, t]).then_inc(s7_st, 16)
            sp.wait_ge(s7_st, 16 * NT)

        @b7.scalar
        def _(act):
            for t in range(NT + 1):
                if t < NT:
                    act.wait_ge(s7_y[t], 32)
                    if t >= 2:
                        act.wait_ge(s7_sum, t - 1)
                    nc.scalar.activation(yw[:, t % 2], y1[:, t], ACT.Copy, scale=w1[:, t:t + 1]).then_inc(s7_w, 1)
                if t:
                    u = t - 1
                    act.wait_ge(s7_x2, u + 1)
                    if u:
                        act.wait_ge(s7_ssq, u)
                    nc.scalar.activation(sq7, x1[:, u], ACT.Square, accum_out=ssq[:, u:u + 1]).then_inc(s7_ssq, 1)
                    act.wait_ge(s7_ssq, u + 1)
                    nc.scalar.activation(rstd[:, u:u + 1], ssq[:, u:u + 1], ACT.Sqrt, bias=epst, scale=1.0 / D
                                         ).then_inc(s7_std, 1)

        @b7.vector
        def _(dve):
            dve.wait_ge(s7_row, 32)
            for t in range(NT + 2):
                if t < NT:
                    dve.wait_ge(s7_y[t], 32)
                    dve.wait_ge(s7_w, t + 1)
                    nc.vector.scalar_tensor_tensor(y2[:, t], y2[:, t], w2[:, t:t + 1], yw[:, t % 2], ALU.mult, ALU.add
                                                   ).then_inc(s7_sum, 1)
                if 1 <= t <= NT:
                    u = t - 1
                    dve.wait_ge(s7_gated, u + 1)
                    nc.vector.tensor_tensor(x1[:, u], x1[:, u], y2[:, u], ALU.add).then_inc(s7_x2, 1)
                if t >= 2:
                    u = t - 2
                    dve.wait_ge(s7_std, u + 1)
                    nc.vector.reciprocal(rstd[:, u:u + 1], rstd[:, u:u + 1]).then_inc(s7_rstd, 1)
                    dve.wait_ge(s7_rstd, u + 1)
                    nc.vector.scalar_tensor_tensor(yo[:, u], x1[:, u], rstd[:, u:u + 1], gainF, ALU.mult, ALU.mult
                                                   ).then_inc(s7_out, 1)

        seventh.close()


_INS = ["x", "c", "ctx", "c_ctx", "mod_w", "mod_b", "norm1_g", "norm2_g", "w_in",
        "conv_dw_w", "conv_dw_b", "conv_ln_g", "conv_ln_b", "conv_pw_w", "conv_pw_b",
        "gdn_conv_w", "gdn_a_log", "gdn_dt_bias", "gdn_norm_g", "attn_q_norm_g", "attn_k_norm_g", "w_out",
        "router_group_w", "router_group_b", "router_expert_w", "router_expert_b",
        "expert_w_gate", "expert_w_up", "expert_w_down", "final_norm_g"]


def kernel(**inputs):
    import numpy as np
    import concourse.bacc as bacc
    from concourse.bass_utils import run_bass_kernel_spmd

    nc = bacc.Bacc("TRN2", target_bir_lowering=False, num_devices=1)
    arrays, args = {}, []
    cst, rope = constants()
    named = [(name, np.ascontiguousarray(inputs[name])) for name in _INS] + [("cst", cst), ("rope", rope)]
    for name, a in named:
        arrays[f"in_{name}"] = a
        args.append(nc.dram_tensor(f"in_{name}", a.shape, mybir.dt.from_np(a.dtype), kind="ExternalInput").ap())
    out = nc.dram_tensor("out", (1, L, D), F32, kind="ExternalOutput").ap()
    trunk(nc, *args, out)
    r = run_bass_kernel_spmd(nc, [arrays], core_ids=[0])
    return r.results[0]["out"]
```
